# Optimizing a Trainium2 kernel written in Bass

```python
import jax, jax.numpy as jnp
from jax import lax
import numpy as np

D_MODEL = 1024
BATCH = 1
SEQ = 128
DEPTH = 1
DEC_BATCH = 1
DEC_SEQ = 512
PAST_LEN = 128

GRID_W = 64
BLOCK = 128
WINDOW = 128
N_HEADS = 8
KV_HEADS = 2
HEAD_DIM = 64
GQA_GROUP = N_HEADS // KV_HEADS
ATTN_WIDTH = N_HEADS * HEAD_DIM
KV_WIDTH = KV_HEADS * HEAD_DIM
GM_HEADS = 8
GM_DIM = 64
GM_WIDTH = GM_HEADS * GM_DIM
CHUNK = 128
MIX_WIDTH = ATTN_WIDTH + GM_WIDTH
IN_WIDTH = ATTN_WIDTH + 2 * KV_WIDTH + 2 * GM_WIDTH
SPLITS = (ATTN_WIDTH, ATTN_WIDTH + KV_WIDTH, ATTN_WIDTH + 2 * KV_WIDTH,
          ATTN_WIDTH + 2 * KV_WIDTH + GM_WIDTH)
ROPE_AXIS_DIM = HEAD_DIM // 2
ROPE_BASE = 10000.0
N_GROUPS = 4
EXPERTS_PER_GROUP = 8
N_EXPERTS = N_GROUPS * EXPERTS_PER_GROUP
TOP_K = 2
D_EXPERT = 256
N_MOD = 6
EPS = 1e-6
NEG_INF = -1e30
SCALE = HEAD_DIM ** -0.5

kernel_name = "hymba_gmlp_hmoe_prefix_dit_step"

def _rms_norm(x, g):
    xf = x.astype(jnp.float32)
    y = xf * lax.rsqrt(jnp.mean(xf * xf, axis=-1, keepdims=True) + EPS)
    return (y * g.astype(jnp.float32)).astype(x.dtype)

def _sink_softmax(s, sink):
    sk = sink.astype(jnp.float32).reshape(KV_HEADS, GQA_GROUP, 1, 1)
    sk = jnp.broadcast_to(sk, s.shape[:-1] + (1,))
    p = jax.nn.softmax(jnp.concatenate([s, sk], axis=-1), axis=-1)
    return p[..., :-1]

def _axial_angles(n_tokens):
    n_rows = n_tokens // GRID_W
    t = jnp.arange(n_rows * GRID_W)
    row = (t // GRID_W).astype(jnp.float32)
    col = (t % GRID_W).astype(jnp.float32)
    inv = jnp.power(ROPE_BASE, -jnp.arange(0, ROPE_AXIS_DIM, 2, dtype=jnp.float32) / ROPE_AXIS_DIM)
    return row[:, None] * inv[None, :], col[:, None] * inv[None, :]

def _rotate(x, ang):
    x1, x2 = jnp.split(x, 2, axis=-1)
    cs = jnp.cos(ang)[None, :, None, :]
    sn = jnp.sin(ang)[None, :, None, :]
    return jnp.concatenate([x1 * cs - x2 * sn, x2 * cs + x1 * sn], axis=-1)

def _axial_rope(x, ang_row, ang_col):
    xf = x.astype(jnp.float32)
    out = jnp.concatenate([_rotate(xf[..., :ROPE_AXIS_DIM], ang_row),
                           _rotate(xf[..., ROPE_AXIS_DIM:], ang_col)], axis=-1)
    return out.astype(x.dtype)

def _context_attention(q, k, v, sink):
    B, C = q.shape[:2]
    qb = jnp.moveaxis(q.reshape(B, C // BLOCK, BLOCK, KV_HEADS, GQA_GROUP, HEAD_DIM), 1, 0)

    def one_block(q_blk):
        s = jnp.einsum('bqhgd,bchd->bhgqc', q_blk, k).astype(jnp.float32) * SCALE
        p = _sink_softmax(s, sink).astype(v.dtype)
        return jnp.einsum('bhgqc,bchd->bqhgd', p, v)

    o = lax.map(one_block, qb)
    return jnp.moveaxis(o, 0, 1).reshape(B, C, ATTN_WIDTH)

def _latent_attention(q, k, v, k_ctx, v_ctx, sink):
    B, L = q.shape[:2]
    nb = L // BLOCK
    qb = jnp.moveaxis(q.reshape(B, nb, BLOCK, KV_HEADS, GQA_GROUP, HEAD_DIM), 1, 0)
    pad = ((0, 0), (BLOCK, BLOCK), (0, 0), (0, 0))
    kp = jnp.pad(k, pad)
    vp = jnp.pad(v, pad)
    qi = jnp.arange(BLOCK)[:, None]
    kj = jnp.arange(3 * BLOCK)[None, :]
    band = jnp.abs(qi + BLOCK - kj) <= WINDOW

    def one_block(args):
        q_blk, n = args
        k_loc = lax.dynamic_slice_in_dim(kp, n * BLOCK, 3 * BLOCK, axis=1)
        v_loc = lax.dynamic_slice_in_dim(vp, n * BLOCK, 3 * BLOCK, axis=1)
        kpos = (n - 1) * BLOCK + kj
        valid = band & (kpos >= 0) & (kpos < L)
        s_loc = jnp.einsum('bqhgd,bmhd->bhgqm', q_blk, k_loc).astype(jnp.float32) * SCALE
        s_loc = jnp.where(valid, s_loc, NEG_INF)
        s_ctx = jnp.einsum('bqhgd,bchd->bhgqc', q_blk, k_ctx).astype(jnp.float32) * SCALE
        p = _sink_softmax(jnp.concatenate([s_loc, s_ctx], axis=-1), sink).astype(v.dtype)
        return (jnp.einsum('bhgqm,bmhd->bqhgd', p[..., :3 * BLOCK], v_loc)
                + jnp.einsum('bhgqc,bchd->bqhgd', p[..., 3 * BLOCK:], v_ctx))

    o = lax.map(one_block, (qb, jnp.arange(nb)))
    return jnp.moveaxis(o, 0, 1).reshape(B, L, ATTN_WIDTH)

def _chunk_gmlp(gu, gv, gm_norm, gm_ws, gm_b):
    B, L, _ = gu.shape
    u = jax.nn.gelu(gu)
    v = _rms_norm(jax.nn.gelu(gv).reshape(B, L, GM_HEADS, GM_DIM), gm_norm)
    vc = v.reshape(B, L // CHUNK, CHUNK, GM_HEADS, GM_DIM)
    vs = jnp.einsum('hpq,bnqhc->bnphc', gm_ws, vc) + jnp.transpose(gm_b)[None, None, :, :, None]
    return u * vs.reshape(B, L, GM_WIDTH)

def _hier_moe(x, router_group, router_expert, w_gate, w_up, w_down):
    B, L, D = x.shape
    t = x.reshape(B * L, D)
    g_prob = jax.nn.softmax((t @ router_group).astype(jnp.float32), axis=-1)
    g_top, g_idx = lax.top_k(g_prob, 1)
    e_logits = (t @ router_expert).astype(jnp.float32).reshape(-1, N_GROUPS, EXPERTS_PER_GROUP)
    g_onehot = jax.nn.one_hot(g_idx[:, 0], N_GROUPS, dtype=jnp.float32)
    e_in_group = jnp.einsum('tge,tg->te', e_logits, g_onehot)
    e_top, e_idx = lax.top_k(e_in_group, TOP_K)
    weights = jax.nn.softmax(e_top, axis=-1) * g_top
    expert_id = g_idx * EXPERTS_PER_GROUP + e_idx
    gates = jnp.sum(jax.nn.one_hot(expert_id, N_EXPERTS, dtype=jnp.float32) * weights[..., None],
                    axis=1).astype(x.dtype)
    hid = jax.nn.silu(jnp.einsum('td,edf->tef', t, w_gate)) * jnp.einsum('td,edf->tef', t, w_up)
    y = jnp.einsum('tef,efd->td', hid * gates[:, :, None], w_down)
    return y.reshape(B, L, D)

def _layer(x, mod, rope, k_ctx, v_ctx, w_in, w_out, attn_sink, gm_norm, gm_ws, gm_b,
           g_pre_mix, g_post_mix, g_pre_ffn, g_post_ffn,
           router_group, router_expert, w_gate, w_up, w_down):
    shift1, scale1, gate1, shift2, scale2, gate2 = jnp.split(mod, N_MOD, axis=-1)
    B, L, _ = x.shape
    h = _rms_norm(x, g_pre_mix) * (1 + scale1) + shift1
    proj = jnp.einsum('bld,de->ble', h, w_in)
    q, k, v, gu, gv = jnp.split(proj, SPLITS, axis=-1)
    q = q.reshape(B, L, N_HEADS, HEAD_DIM)
    k = k.reshape(B, L, KV_HEADS, HEAD_DIM)
    v = v.reshape(B, L, KV_HEADS, HEAD_DIM)
    if rope is None:
        attn = _context_attention(q, k, v, attn_sink)
    else:
        attn = _latent_attention(_axial_rope(q, *rope), _axial_rope(k, *rope), v, k_ctx, v_ctx, attn_sink)
    gm = _chunk_gmlp(gu, gv, gm_norm, gm_ws, gm_b)
    mix = jnp.einsum('ble,ed->bld', jnp.concatenate([attn, gm], axis=-1), w_out)
    x = x + gate1 * _rms_norm(mix, g_post_mix)
    h2 = _rms_norm(x, g_pre_ffn) * (1 + scale2) + shift2
    f = _hier_moe(h2, router_group, router_expert, w_gate, w_up, w_down)
    x = x + gate2 * _rms_norm(f, g_post_ffn)
    return x, k, v

def setup_inputs(seed: int = 0) -> dict:
    key = jax.random.key(seed)
    ks = jax.random.split(key, 23)

    def nrm(k, shape, scale):
        return jax.random.normal(k, shape, jnp.float32) * scale

    return {
        "x_prompt": nrm(ks[0], (BATCH, SEQ, D_MODEL), 1.0),
        "x_sample": nrm(ks[1], (DEC_BATCH, DEC_SEQ, D_MODEL), 1.0),
        "cache_k": nrm(ks[2], (DEC_BATCH, DEPTH, PAST_LEN, KV_HEADS, HEAD_DIM), 1.0),
        "cache_v": nrm(ks[3], (DEC_BATCH, DEPTH, PAST_LEN, KV_HEADS, HEAD_DIM), 1.0),
        "c": nrm(ks[4], (DEC_BATCH, D_MODEL), 1.0),
        "c_ctx": nrm(ks[5], (D_MODEL,), 0.5),
        "w_mod": nrm(ks[6], (DEPTH, D_MODEL, N_MOD * D_MODEL), 0.5 * D_MODEL ** -0.5),
        "b_mod": nrm(ks[7], (DEPTH, N_MOD * D_MODEL), 0.01),
        "g_pre_mix": 1.0 + nrm(ks[8], (DEPTH, D_MODEL), 0.05),
        "w_in": nrm(ks[9], (DEPTH, D_MODEL, IN_WIDTH), D_MODEL ** -0.5),
        "attn_sink": nrm(ks[10], (DEPTH, N_HEADS), 0.5),
        "gm_norm": 1.0 + nrm(ks[11], (DEPTH, GM_HEADS, GM_DIM), 0.05),
        "gm_ws": nrm(ks[12], (DEPTH, GM_HEADS, CHUNK, CHUNK), CHUNK ** -0.5),
        "gm_b": 1.0 + nrm(ks[13], (DEPTH, GM_HEADS, CHUNK), 0.05),
        "w_out": nrm(ks[14], (DEPTH, MIX_WIDTH, D_MODEL), MIX_WIDTH ** -0.5),
        "g_post_mix": 1.0 + nrm(ks[15], (DEPTH, D_MODEL), 0.05),
        "g_pre_ffn": 1.0 + nrm(ks[16], (DEPTH, D_MODEL), 0.05),
        "router_group": nrm(ks[17], (DEPTH, D_MODEL, N_GROUPS), D_MODEL ** -0.5),
        "router_expert": nrm(ks[18], (DEPTH, D_MODEL, N_EXPERTS), D_MODEL ** -0.5),
        "w_gate": nrm(ks[19], (DEPTH, N_EXPERTS, D_MODEL, D_EXPERT), D_MODEL ** -0.5),
        "w_up": nrm(ks[20], (DEPTH, N_EXPERTS, D_MODEL, D_EXPERT), D_MODEL ** -0.5),
        "w_down": nrm(ks[21], (DEPTH, N_EXPERTS, D_EXPERT, D_MODEL), D_EXPERT ** -0.5),
        "g_post_ffn": 1.0 + nrm(ks[22], (DEPTH, D_MODEL), 0.05),
    }

def reference(x_prompt, x_sample, cache_k, cache_v, c, c_ctx, w_mod, b_mod, g_pre_mix, w_in,
              attn_sink, gm_norm, gm_ws, gm_b, w_out, g_post_mix, g_pre_ffn,
              router_group, router_expert, w_gate, w_up, w_down, g_post_ffn):
    x = x_prompt
    ks, vs = [], []
    for l in range(DEPTH):
        lp = (w_in[l], w_out[l], attn_sink[l], gm_norm[l], gm_ws[l], gm_b[l],
              g_pre_mix[l], g_post_mix[l], g_pre_ffn[l], g_post_ffn[l],
              router_group[l], router_expert[l], w_gate[l], w_up[l], w_down[l])
        mod = jax.nn.silu(c_ctx) @ w_mod[l] + b_mod[l]
        x, k, v = _layer(x, mod, None, None, None, *lp)
        ks.append(k)
        vs.append(v)
    y_prompt = x
    new_k = jnp.stack(ks, axis=1)
    new_v = jnp.stack(vs, axis=1)

    rope = _axial_angles(x_sample.shape[1])
    x = x_sample
    for l in range(DEPTH):
        lp = (w_in[l], w_out[l], attn_sink[l], gm_norm[l], gm_ws[l], gm_b[l],
              g_pre_mix[l], g_post_mix[l], g_pre_ffn[l], g_post_ffn[l],
              router_group[l], router_expert[l], w_gate[l], w_up[l], w_down[l])
        mod = (jax.nn.silu(c) @ w_mod[l] + b_mod[l])[:, None, :]
        x, _, _ = _layer(x, mod, rope, cache_k[:, l], cache_v[:, l], *lp)
    y_sample = x
    return (y_prompt, y_sample, new_k, new_v)


_drawn_inputs = setup_inputs


def setup_inputs(seed=0):
    import zlib

    import numpy as np

    out = dict(_drawn_inputs(seed))
    spreads = {}
    factors = {'attn_sink': 8.0, 'g_post_ffn': 4.129}
    for name, (base, spread) in spreads.items():
        noise = np.random.default_rng([zlib.crc32(name.encode()), seed]).standard_normal(out[name].shape)
        drawn = base * np.exp(spread * noise) if base else spread * noise
        out[name] = __import__('jax').numpy.asarray(drawn.astype(out[name].dtype))
    for name, factor in factors.items():
        out[name] = (out[name] * factor).astype(out[name].dtype)
    return out
```

```python
from contextlib import ExitStack

import concourse.bass as bass
from concourse import mybir

ALU = mybir.AluOpType
ACT = mybir.ActivationFunctionType
F32 = mybir.dt.float32
BF16 = mybir.dt.bfloat16
F16 = mybir.dt.float16
I32 = mybir.dt.int32
U32 = mybir.dt.uint32
AX_X = mybir.AxisListType.X

P = 128
D = 1024
KC = D // P
CTX, LAT = 128, 512
TILES = (CTX + LAT) // P
HEADS, KVH, HD = 8, 2, 64
PAIRS = HEADS // KVH
ATT = HEADS * HD
KVW = KVH * HD
QKV = ATT + 2 * KVW
GMH, GMD = 8, 64
GM = GMH * GMD
N_MOD = 6
GROUPS, EPG = 4, 8
EXPERTS = GROUPS * EPG
FE = 256
TOPK = 2
SLOT = 64
MAX_EXTRA = (TOPK * (CTX + LAT) - 1) // SLOT
MAX_TILES = EXPERTS + MAX_EXTRA
EPS = 1e-6
SCALE = HD ** -0.5
NEG = -1e30

RING = 4
SLOT_ELEMS = 3 * KC * FE
MB = 768
N_MB = N_MOD * D // MB
MB_CHUNKS = MB // P

CONST_COLS = {}
_at = 0
for _name, _n in (("ident", P), ("slot", P), ("tile", MAX_TILES), ("token", TILES), ("half", 1),
                  ("cos", 4 * HD), ("sin", 4 * HD), ("before", P), ("mask_prev", P), ("mask_next", P)):
    CONST_COLS[_name] = (_at, _at + _n)
    _at += _n
N_CONST = _at
N_KEPT = CONST_COLS["before"][0]

ROWS = {}
_at = 0
for _name, _n in (("b_mod", N_MOD * KC), ("pre_mix", KC), ("post_mix", KC), ("pre_ffn", KC),
                  ("post_ffn", KC), ("gm_b", GMH)):
    ROWS[_name] = (_at, _at + _n)
    _at += _n
N_ROWS = _at


def constants():
    import numpy as np
    c = np.zeros((P, N_CONST), np.float32)

    def put(name, value):
        a, b = CONST_COLS[name]
        c[:, a:b] = np.asarray(value, np.float32).reshape(P, b - a)

    i = np.arange(P)
    put("ident", np.eye(P))
    put("before", i[:, None] < i[None, :])
    put("mask_prev", np.where(i[None, :] >= i[:, None], 0.0, NEG))
    put("mask_next", np.where(i[None, :] <= i[:, None], 0.0, NEG))
    put("slot", np.broadcast_to(i[None, :] % SLOT, (P, P)))
    put("tile", np.broadcast_to(np.arange(MAX_TILES)[None, :], (P, MAX_TILES)))
    put("token", 2.0 * (i[:, None] + P * np.arange(TILES)[None, :]))
    put("half", i // SLOT)
    t = np.arange(LAT)
    inv = np.power(np.float32(10000.0), -np.arange(0, 32, 2, dtype=np.float32) / np.float32(32))
    inv = inv.astype(np.float32)
    row = (t // 64).astype(np.float32)[:, None] * inv[None, :]
    col = (t % 64).astype(np.float32)[:, None] * inv[None, :]
    cos = np.concatenate([np.cos(row), np.cos(row), np.cos(col), np.cos(col)], 1)
    sin = np.concatenate([np.sin(row), -np.sin(row), np.sin(col), -np.sin(col)], 1)
    put("cos", cos.reshape(4, P, HD).transpose(1, 0, 2))
    put("sin", sin.reshape(4, P, HD).transpose(1, 0, 2))
    return c


def hybrid_dit_step(
    nc, x_prompt, x_sample, cache_k, cache_v, c, c_ctx, w_mod, b_mod, g_pre_mix, w_in, attn_sink,
    gm_norm, gm_ws, gm_b, w_out, g_post_mix, g_pre_ffn, router_group, router_expert, w_gate, w_up,
    w_down, g_post_ffn, consts, y_prompt, y_sample, new_k, new_v,
):
    with ExitStack() as ctx:
        def sem(name):
            return ctx.enter_context(nc.semaphore(name))

        base = (nc.sbuf_base + 31) // 32 * 32
        at = [base]

        def sb(name, shape, dt, offset=None):
            size = 4 if dt in (F32, I32, U32) else 2
            n = size
            for s in shape[1:]:
                n *= s
            n = (n + 31) // 32 * 32
            if offset is None:
                offset = at[0]
                at[0] += n
            return nc.alloc_sbuf_tensor_at(name, list(shape), dt, offset=offset)

        def region(n):
            o = at[0]
            at[0] += n
            return o

        KB = 1024
        ring = sb("ring", [P, RING, SLOT_ELEMS], F32)
        cst = sb("cst", [P, N_KEPT], F32)
        cols = sb("cols", [P, N_ROWS], F32)
        gate_bc = sb("gate_bc", [P, 2, 2, D], F32)
        res_at = region(20 * KB)
        res = sb("res", [P, TILES, D], F32, res_at)
        mod = sb("mod", [P, N_MOD * KC, 2], F32)
        pre = sb("pre", [P, 2, 2, KC, 2], F32)
        post = sb("post", [P, 2, KC, 2], F32)
        cond_in = sb("cond_in", [P, KC, 2], F32)
        cond = sb("cond", [P, KC, 32], F32)
        stats = sb("stats", [P, 8, 8], F32)
        gm_stats = sb("gm_stats", [P, 3, TILES * GMH], F32)
        att_stats = sb("att_stats", [P, 8, TILES * PAIRS, 2], F32)
        nsink = sb("nsink", [P, HEADS], F32)
        sink = sb("sink", [P, HEADS], F32)
        half_pow = sb("half_pow", [P, TILES * GMH], F32)
        ident_b = sb("ident_b", [P, P], BF16)
        ones_b = sb("ones_b", [P, P], BF16)
        before_b = sb("before_b", [P, P], BF16)
        mask_b = sb("mask_b", [P, 2, P], BF16)
        w_r = sb("w_r", [P, KC, GROUPS + EXPERTS], F32)
        tile_src = sb("tile_src", [P, MAX_TILES], U32)
        extra_at = sb("extra_at", [P, EXPERTS + 1], I32)
        back_row = sb("back_row", [P, TILES, TOPK], U32)
        w_tok = sb("w_tok", [P, TILES, TOPK], F32)
        a0 = region(20 * KB)
        h_t = sb("h_t", [P, KC, TILES * P], F32, a0)
        mix_t = sb("mix_t", [P, KC, TILES * P], F32, a0)
        xg = sb("xg", [P, 4, 512], F32, a0)
        xt = sb("xt", [P, 2, 4, P], F32, a0 + 8 * KB)
        act_g = sb("act_g", [P, 2, P], F32, a0 + 12 * KB)
        hid = sb("hid", [P, 2, P], F32, a0 + 13 * KB)
        hid_t = sb("hid_t", [P, 2, P], F32, a0 + 14 * KB)
        y_sb = sb("y_sb", [P, 2, 512], F32, a0 + 15 * KB)
        idx_col = sb("idx_col", [P, 4, 8], U32, a0 + 19 * KB)
        b0 = region(10 * KB)
        cst_once = sb("cst_once", [P, N_CONST - N_KEPT], F32, b0)
        rows = sb("rows", [N_ROWS, P], F32, b0 + 2 * KB)
        gm_u = sb("gm_u", [P, TILES, GM], F32, b0)
        probs = sb("probs", [P, 2, 2, 512], F32, b0)
        h2 = sb("h2", [P, 2, D], F32, b0)
        xg_x = sb("xg_x", [P, 512], F32, b0)
        xt_x = sb("xt_x", [P, 4, P], F32, b0 + 2 * KB)
        act_x = sb("act_x", [P, P], F32, b0 + 4 * KB)
        hid_x = sb("hid_x", [P, P], F32, b0 + 4 * KB + 512)
        hid_tx = sb("hid_tx", [P, P], F32, b0 + 5 * KB)
        y_x = sb("y_x", [P, 512], F32, b0 + 6 * KB)
        idx_x = sb("idx_x", [P, 8], U32, b0 + 8 * KB)
        c0 = region(10 * KB)
        q_t = sb("q_t", [P, PAIRS, TILES * P], F32, c0)
        h2_t = sb("h2_t", [P, 2, KC, P], F32, c0)
        d0 = region(9 * KB)
        k_t = sb("k_t", [P, KVH, 6 * P], F32, d0)
        v_all = sb("v_all", [P, 6, KVW], F32, d0 + 6 * KB)
        one_hot = sb("one_hot", [P, TILES, TOPK, EXPERTS], F32, d0)
        r_prod = sb("r_prod", [P, TILES * GROUPS * EPG * TOPK], F32, d0 + 1280)
        both = sb("both", [P, TILES, EXPERTS], BF16, d0 + 2560)
        r_s = sb("r_s", [P, 32, TILES, TOPK], F32, d0 + 3 * KB)
        r_8 = sb("r_8", [P, 3, TILES, 8], F32, d0 + 4352)
        r_i8 = sb("r_i8", [P, 2, TILES, 8], U32, d0 + 4864)
        r_e = sb("r_e", [P, 4, EXPERTS + 1], F32, d0 + 5184)
        r_ei = sb("r_ei", [P, EXPERTS], I32, d0 + 5728)
        r_i = sb("r_i", [P, 3, TILES, TOPK], I32, d0 + 5888)
        sel_tile = sb("sel_tile", [P, TILES * TOPK, MAX_TILES], F16, d0 + 6016)
        logits = sb("logits", [P, TILES, GROUPS + EXPERTS], F32, d0 + 7104)
        t0 = region(16 * KB)
        part = sb("part", [P, 2, MB], F32, t0)
        qk_rot = sb("qk_rot", [P, 2, ATT + KVW], F32, t0 + 6 * KB)
        qk_sin = sb("qk_sin", [P, ATT + KVW], F32, t0 + 11 * KB)
        k_raw = sb("k_raw", [P, 2, KVW], F32, t0 + 13 * KB + 512)
        cache_sb = sb("cache_sb", [P, KVW], F32, t0 + 14 * KB + 512)
        junk_1 = sb("junk_1", [P, D], F32, c0)
        junk_2 = sb("junk_2", [P, D], F32, d0)
        sq = sb("sq", [P, 2, GM], F32, t0)
        p_t = sb("p_t", [P, 2, KVH, 4, 2, P], F32, t0)
        mix_g = sb("mix_g", [P, 2, D], F32, t0)
        xn2 = sb("xn2", [P, D], F32, t0 + 8 * KB)
        lg_t = sb("lg_t", [GROUPS + EXPERTS, P], F32, t0 + 12 * KB)
        sel_slot = sb("sel_slot", [P, TILES * TOPK, P], F16, t0 + 13 * KB)
        gm_v = sb("gm_v", [P, TILES, GM], F32, res_at)
        zeros = sb("zeros", [P, 512], F32, res_at + 10 * KB)
        ws_raw = sb("ws_raw", [P, GMH, P], F32, t0 + 4 * KB)
        ws_t = sb("ws_t", [P, GMH, P], F32, t0 + 8 * KB)
        gmn_bc = sb("gmn_bc", [P, GM], F32, t0 + 12 * KB)
        ring_at = base
        y_back = sb("y_back", [P, TILES, TOPK, D], F32, ring_at)
        y_sum = sb("y_sum", [P, 2, D], F32, ring_at + 40 * KB)
        y_out = sb("y_out", [P, 2, D], F32, ring_at + 48 * KB)
        junk_3 = sb("junk_3", [P, D], F32, ring_at + 56 * KB)
        assert at[0] <= nc.sbuf_usable_end, (at[0], nc.sbuf_usable_end)

        def const(name):
            a, b = CONST_COLS[name]
            return cst[:, a:b] if b <= N_KEPT else cst_once[:, a - N_KEPT:b - N_KEPT]

        ident = const("ident")

        ps = ctx.enter_context(nc.psum_tensor("ps", [P, 8, 512], F32))

        h2_dram = nc.dram_tensor("h2_rows", [TILES * P, D], F32, kind="Internal").ap()
        y_dram = nc.dram_tensor("y_slots", [MAX_TILES, SLOT, D], F32, kind="Internal").ap()
        h2_halves = h2_dram.rearrange("t (h n) -> (t h) n", h=2)
        y_rows = y_dram.rearrange("a s n -> (a s) n")

        s_const, s_rows, s_cond, s_xp, s_xs, s_small = (sem(n) for n in (
            "const_in", "rows_in", "cond_in", "xp_in", "xs_in", "small_in"))
        s_cache, s_wr, s_ws, s_gmn = (sem(n) for n in ("cache_in", "wr_in", "ws_in", "gmn_in"))
        ring_in = [sem(f"ring_in{i}") for i in range(RING)]
        s_zero, s_b16, s_cst2 = sem("zeroed"), sem("consts_cast"), sem("consts_made")
        dve_link, pool_link, act_link = sem("dve_link"), sem("pool_link"), sem("act_link")
        s_silu, s_colps, s_cols = sem("cond_silu"), sem("cols_ps"), sem("cols_made")
        s_sq1, s_ms1, s_rs1, s_xn = sem("sq1"), sem("ms1"), sem("rs1"), sem("xn")
        mod_mm, mod_part, mod_tr, mod_col = sem("mod_mm"), sem("mod_part"), sem("mod_tr"), sem("mod_col")
        s_pre1, s_pre2 = sem("pre1_made"), sem("pre2_made")
        ht_tr, ht_dve, ht_act = sem("ht_tr"), sem("ht_dve"), sem("ht_act")
        qkv_mm, q_read, kv_read, rot_done = sem("qkv_mm"), sem("q_read"), sem("kv_read"), sem("rot_done")
        qk_tr, qk_act, qk_dve, s_newkv = sem("qk_tr"), sem("qk_act"), sem("qk_dve"), sem("newkv_out")
        gu_mm, gelu_done, gsq_done, gv_rs, gv_ms = (
            sem("gu_mm"), sem("gelu_done"), sem("gsq_done"), sem("gv_rs"), sem("gv_ms"))
        gv_red, gv_scaled, gv_ready = sem("gv_red"), sem("gv_scaled"), sem("gv_ready")
        ws_tr, ws_cp, gm_mm, gm_done, gm_tr, gm_cp = (
            sem("ws_tr"), sem("ws_cp"), sem("gm_mm"), sem("gm_done"), sem("gm_tr"), sem("gm_cp"))
        gate_mm, gate_cp = sem("gate_mm"), sem("gate_cp")
        s_post = sem("post_made")
        score_mm, neg_max, sink_arg, exp_done, inv_sum, p_norm = (
            sem("score_mm"), sem("neg_max"), sem("sink_arg"), sem("exp_done"), sem("inv_sum"), sem("p_norm"))
        pt_tr, pt_even, pt_odd, pv_mm, pv_cp = (
            sem("pt_tr"), sem("pt_even"), sem("pt_odd"), sem("pv_mm"), sem("pv_cp"))
        s_xre, s_filled = sem("x_again"), sem("extra_slots_filled")
        op_mm, sq2, ms2, rs2, mixg, res1, sq3, ms3, rs3, xn2_done = (
            sem(n) for n in ("op_mm", "sq2", "ms2", "rs2", "mixg", "res1", "sq3", "ms3", "rs3", "xn2_done"))
        t2_tr, t2_dve, t2_act, t2_back, h2_dve, h2_act = (
            sem(n) for n in ("t2_tr", "t2_dve", "t2_act", "t2_back", "h2_dve", "h2_act"))
        h2_out = [sem("h2_out0"), sem("h2_out1")]
        rt_mm, rt_cp, rt_tr, rt_lg = sem("rt_mm"), sem("rt_cp"), sem("rt_tr"), sem("rt_lg")
        r_sub, r_exp, r_both, r_pos, r_sel, r_idx, r_ready = (
            sem(n) for n in ("r_sub", "r_exp", "r_both", "r_pos", "r_sel", "r_idx", "r_ready"))
        xg_in = [sem(f"xg_in{i}") for i in range(4)]
        x_tr, x_cp, gu2_mm, silu_done, hid_done, ht2_tr, ht2_cp, y_mm, y_cp = (
            sem(n) for n in ("x_tr", "x_cp", "gu2_mm", "silu_done", "hid_done", "ht2_tr", "ht2_cp", "y_mm", "y_cp"))
        y_st = [sem("y_st0"), sem("y_st1")]
        expert_done, idx_cp, idx_seen = sem("expert_done"), sem("idx_cp"), sem("idx_seen")
        e_in, e_idx, e_tr, e_cp, e_gu, e_silu, e_hid, e_htr, e_htc, e_y, e_yc, e_st, e_all = (
            sem("extra_" + n) for n in ("in", "idx", "tr", "cp", "gu", "silu", "hid", "htr", "htc",
                                        "y", "yc", "st", "all"))
        back_in = [sem(f"back_in{i}") for i in range(TILES)]
        f_sum, f_sq, f_ms, f_rs, f_gated, f_out = (
            sem("fin_" + n) for n in ("sum", "sq", "ms", "rs", "gated", "out"))
        f_st = [sem("fin_st0"), sem("fin_st1")]

        ITEMS = ["m0", "m1", "m2", "qkv", "m3", "gu", "m4", "gv", "m5", "m6", "m7", "wo0", "wo1"]
        N_FIRST = len(ITEMS)
        DMAS = [3 if i.startswith("wo") else 1 for i in ITEMS]
        USED = {f"m{b}": (mod_mm, b + 1) for b in range(N_MB)}
        USED.update({"qkv": (qkv_mm, TILES), "gu": (gu_mm, TILES), "gv": (gu_mm, 2 * TILES),
                     "wo0": (op_mm, TILES), "wo1": (op_mm, TILES)})

        def slot_of(r):
            return r % RING

        def landed(r):
            return 16 * sum(DMAS[i] for i in range(r % RING, r + 1, RING))

        def expert_base(slot):
            return 16 * sum(DMAS[i] for i in range(slot, N_FIRST, RING))

        def item(name):
            r = ITEMS.index(name)
            return ring[:, slot_of(r), :], ring_in[slot_of(r)], landed(r)

        GROUP_OF = lambda j: (N_FIRST + j) % RING

        def cond_of(i):
            return 0 if i == 0 else 1

        x_lat = x_sample[0].rearrange("(t p) d -> p t d", p=P)

        block = ctx.enter_context(nc.Block())

        @block.sync
        def _(sp):
            sp.dma_start(cst[:], consts[:, 0:N_KEPT]).then_inc(s_const, 16)
            sp.dma_start(cst_once[:], consts[:, N_KEPT:]).then_inc(s_const, 16)
            sp.dma_start(cond_in[:, :, 0], c_ctx.rearrange("(p k) -> p k", k=KC),
                         allow_slow_non_contiguous=True).then_inc(s_cond, 16)
            sp.dma_start(cond_in[:, :, 1], c[0].rearrange("(p k) -> p k", k=KC),
                         allow_slow_non_contiguous=True).then_inc(s_cond, 16)
            sp.dma_start(res[:, 0, :], x_prompt[0]).then_inc(s_xp, 16)
            sp.dma_start(res[:, 1:TILES, :], x_lat).then_inc(s_xs, 16)
            for r, name in enumerate(ITEMS):
                if r >= RING:
                    s, v = USED[ITEMS[r - RING]]
                    sp.wait_ge(s, v)
                dst, done = ring[:, slot_of(r), :], ring_in[slot_of(r)]
                if name[0] == "m":
                    b = int(name[1])
                    sp.dma_start(dst.rearrange("p (k f) -> p k f", k=KC),
                                 w_mod[0, :, b * MB:(b + 1) * MB].rearrange("(p k) f -> p k f", k=KC)
                                 ).then_inc(done, 16)
                elif name in ("qkv", "gu", "gv"):
                    a, n = {"qkv": (0, QKV), "gu": (QKV, GM), "gv": (QKV + GM, GM)}[name]
                    sp.dma_start(dst[:, 0:KC * n].rearrange("p (k f) -> p k f", k=KC),
                                 w_in[0, :, a:a + n].rearrange("(k p) f -> p k f", p=P)).then_inc(done, 16)
                else:
                    a = 512 * int(name[2])
                    v = dst[:, 0:KC * 512].rearrange("p (k f) -> p k f", k=KC)
                    for kv in range(KVH):
                        sp.dma_start(v[kv * HD:(kv + 1) * HD, 0:PAIRS, :],
                                     w_out[0, kv * PAIRS * HD:(kv + 1) * PAIRS * HD, a:a + 512]
                                     .rearrange("(g d) n -> d g n", d=HD)).then_inc(done, 16)
                    sp.dma_start(v[:, PAIRS:KC, :],
                                 w_out[0, ATT:, a:a + 512].rearrange("(k p) n -> p k n", p=P)).then_inc(done, 16)

            def load_expert(e, j):
                dst, done = ring[:, GROUP_OF(j), :], ring_in[GROUP_OF(j)]
                n = KC * FE
                sp.dma_start(dst[:, 0:n].rearrange("p (k f) -> p k f", k=KC),
                             w_gate[0, e].rearrange("(k p) f -> p k f", p=P)).then_inc(done, 16)
                sp.dma_start(dst[:, n:2 * n].rearrange("p (k f) -> p k f", k=KC),
                             w_up[0, e].rearrange("(k p) f -> p k f", p=P)).then_inc(done, 16)
                sp.dma_start(dst[:, 2 * n:3 * n].rearrange("p (k f) -> p k f", k=2),
                             w_down[0, e].rearrange("(k p) f -> p k f", p=P)).then_inc(done, 16)

            for j in range(RING):
                s, v = USED[ITEMS[N_FIRST + j - RING]]
                sp.wait_ge(s, v)
                load_expert(j, j)
            with sp.Fori(1, EXPERTS // RING) as it:
                for j in range(RING):
                    e = it * RING + j
                    sp.wait_ge(y_mm, e - RING + 1)
                    sp.wait_ge(expert_done, e - RING + 1)
                    load_expert(e, j)

        @block.tensor
        def _(pe):
            def transpose(out, in_, n_in=P):
                return pe.matmul(out, in_, ident[0:n_in, 0:n_in], is_transpose=True, start=True, stop=True)

            pe.wait_ge(s_const, 32)
            pe.wait_ge(s_rows, 96)
            transpose(ps[:, 3, 256:256 + N_ROWS], rows[:, :], N_ROWS)
            pe.wait_ge(s_cache, 32)
            transpose(ps[:, 3, 128:256], cache_sb[:, :]).then_inc(s_colps, 1)
            pe.wait_ge(s_silu, 1)

            def mod_block(b):
                w, s, v = item(f"m{b}")
                w = w.rearrange("p (k f) -> p k f", k=KC)
                pe.wait_ge(s, v)
                if b:
                    pe.wait_ge(mod_part, b)
                for hh in range(2):
                    for k in range(KC):
                        g = k % 4
                        last = pe.matmul(ps[32 * g:32 * g + 32, hh, 0:MB // 2], cond[:, k, :],
                                         w[:, k, hh * (MB // 2):(hh + 1) * (MB // 2)],
                                         start=(k < 4), stop=(k >= 4))
                last.then_inc(mod_mm, 1)

            def mod_turn(b):
                pe.wait_ge(mod_part, b + 1)
                if b:
                    pe.wait_ge(mod_col, b)
                else:
                    pe.wait_ge(s_cols, 1)
                if b == 3:
                    pe.wait_ge(qk_act, TILES)
                    pe.wait_ge(qk_dve, TILES)
                for j in range(MB_CHUNKS):
                    last = transpose(ps[:, 2 + j // 4, (j % 4) * P:(j % 4 + 1) * P],
                                     part[:, b % 2, j * P:(j + 1) * P])
                last.then_inc(mod_tr, 1)

            for b in range(3):
                mod_block(b)
                mod_turn(b)

            for i in range(TILES):
                pe.wait_ge(s_xn, i + 1)
                if i >= 2:
                    pe.wait_ge(ht_dve, i - 1)
                    pe.wait_ge(ht_act, i - 1)
                for k in range(KC):
                    last = transpose(ps[:, 4 + 2 * (i % 2) + k // 4, (k % 4) * P:(k % 4 + 1) * P],
                                     res[:, i, k * P:(k + 1) * P])
                last.then_inc(ht_tr, 1)

            def turn_qk(i):
                pe.wait_ge(rot_done, i + 1)
                if i == 0:
                    pe.wait_ge(mod_col, 3)
                else:
                    pe.wait_ge(qk_act, i)
                    pe.wait_ge(qk_dve, i)
                for g in range(PAIRS):
                    transpose(ps[:, 2, g * P:(g + 1) * P], qk_rot[:, i % 2, g * P:(g + 1) * P])
                transpose(ps[:, 3, 0:P], qk_rot[:, i % 2, ATT:]).then_inc(qk_tr, 1)

            w, s, v = item("qkv")
            w = w.rearrange("p (k f) -> p k f", k=KC)
            pe.wait_ge(s, v)
            for i in range(TILES):
                if i < 2:
                    pe.wait_ge(ht_dve, TILES)
                    pe.wait_ge(ht_act, TILES)
                else:
                    pe.wait_ge(q_read, i - 1)
                    pe.wait_ge(kv_read, i - 1)
                for k in range(KC):
                    h = h_t[:, k, i * P:(i + 1) * P]
                    pe.matmul(ps[:, 4 + 2 * (i % 2), 0:ATT], h, w[:, k, 0:ATT], start=(k == 0), stop=(k == KC - 1))
                    last = pe.matmul(ps[:, 5 + 2 * (i % 2), 0:2 * KVW], h, w[:, k, ATT:QKV],
                                     start=(k == 0), stop=(k == KC - 1))
                last.then_inc(qkv_mm, 1)
                if i:
                    turn_qk(i - 1)

            def gate_proj(u0, name):
                w, s, v = item(name)
                w = w[:, 0:KC * GM].rearrange("p (k f) -> p k f", k=KC)
                pe.wait_ge(s, v)
                for i in range(TILES):
                    u = u0 + i
                    if u >= 4:
                        pe.wait_ge(gelu_done, u - 3)
                    else:
                        pe.wait_ge(q_read, TILES)
                        pe.wait_ge(kv_read, TILES)
                    for k in range(KC):
                        last = pe.matmul(ps[:, 4 + u % 4, :], h_t[:, k, i * P:(i + 1) * P], w[:, k, :],
                                         start=(k == 0), stop=(k == KC - 1))
                    last.then_inc(gu_mm, 1)
                    if i == 0 and u0 == 0:
                        turn_qk(TILES - 1)

            mod_block(3)
            gate_proj(0, "gu")
            mod_turn(3)
            mod_block(4)
            mod_turn(4)
            gate_proj(TILES, "gv")
            for b in range(5, N_MB):
                mod_block(b)
                mod_turn(b)

            pe.wait_ge(s_post, 1)
            pe.wait_ge(mod_col, N_MB)
            for sub in range(2):
                if sub:
                    pe.wait_ge(gate_cp, 1)
                for cnd in range(2):
                    for k in range(KC):
                        col = post[:, sub, k, cnd:cnd + 1].broadcast_to((P, P))
                        last = pe.matmul(ps[:, 2 * cnd + k // 4, (k % 4) * P:(k % 4 + 1) * P], col, ident,
                                         start=(k % 4 == 0), stop=(k % 4 == 3))
                last.then_inc(gate_mm, 1)

            pe.wait_ge(gate_cp, 2)
            pe.wait_ge(s_ws, 16)
            for h in range(GMH):
                last = transpose(ps[:, h // 4, (h % 4) * P:(h % 4 + 1) * P], ws_raw[:, h, :])
            last.then_inc(ws_tr, 1)
            pe.wait_ge(ws_cp, 1)
            pe.wait_ge(gv_ready, TILES)
            for h in range(GMH):
                if h >= 4:
                    pe.wait_ge(gm_done, h - 3)
                pe.matmul(ps[:, 4 + h % 4, 0:TILES * GMD].rearrange("p (t c) -> p t c", t=TILES), ws_t[:, h, :],
                          gm_v[:, :, h * GMD:(h + 1) * GMD], start=True, stop=True).then_inc(gm_mm, 1)
            for i in range(TILES):
                pe.wait_ge(gm_done, GMH)
                if i >= 4:
                    pe.wait_ge(gm_cp, i - 3)
                for cc in range(4):
                    last = transpose(ps[:, 4 + i % 4, cc * P:(cc + 1) * P], gm_u[:, i, cc * P:(cc + 1) * P])
                last.then_inc(gm_tr, 1)

            def chunks(i):
                if i == 0:
                    return [5]
                n = i - 1
                return [0] + [1 + m for m in range(max(n - 1, 0), min(n + 2, 4))]

            def scores(t):
                i, g = t // PAIRS, t % PAIRS
                ch = chunks(i)
                q = q_t[:, g, i * P:(i + 1) * P]
                for a in range(KVH):
                    bank = ps[:, 2 * (t % 2) + a, :]
                    n = P * len(ch)
                    parts = [(0, ch[0], len(ch))] if i <= 1 else [(0, 0, 1), (1, ch[1], len(ch) - 1)]
                    masks = []
                    if i >= 2:
                        masks.append((1, 0))
                    if 1 <= i <= 3:
                        masks.append((len(ch) - 1, 1))
                    for z, (pos, first, cnt) in enumerate(parts):
                        last = pe.matmul(bank[:, pos * P:(pos + cnt) * P], q, k_t[:, a, first * P:(first + cnt) * P],
                                         start=(z == 0), stop=(z == len(parts) - 1 and not masks),
                                         skip_group_check=True)
                    for z, (pos, m) in enumerate(masks):
                        last = pe.matmul(bank[:, pos * P:(pos + 1) * P], ident_b[:, :], mask_b[:, m, :],
                                         start=False, stop=(z == len(masks) - 1), skip_group_check=True)
                last.then_inc(score_mm, 1)

            def turn_p(t):
                i = t // PAIRS
                pe.wait_ge(p_norm, t + 1)
                for a in range(KVH):
                    u = 2 * t + a
                    if u >= 3:
                        pe.wait_ge(pt_odd if (u - 3) % 2 else pt_even, (u - 3) // 2 + 1)
                    for x in range(len(chunks(i))):
                        last = transpose(ps[:, 5 + u % 3, x * P:(x + 1) * P], probs[:, t % 2, a, x * P:(x + 1) * P])
                    last.then_inc(pt_tr, 1)

            def values(m):
                i = m // 2
                ch = chunks(i)
                pe.wait_ge(pt_even, 2 * m + 2)
                pe.wait_ge(pt_odd, 2 * m + 2)
                if m:
                    pe.wait_ge(pv_cp, m)
                for x, cc in enumerate(ch):
                    for a in range(KVH):
                        last = pe.matmul(ps[a * HD:(a + 1) * HD, 4, 0:2 * P], v_all[:, cc, a * HD:(a + 1) * HD],
                                         p_t[:, m % 2, a, x].rearrange("p g q -> p (g q)"),
                                         start=(x == 0), stop=(x == len(ch) - 1))
                last.then_inc(pv_mm, 1)

            NT = TILES * PAIRS
            pe.wait_ge(qk_act, TILES)
            pe.wait_ge(qk_dve, TILES)
            pe.wait_ge(s_b16, 1)
            pe.wait_ge(gm_cp, TILES)
            for t in range(NT + 3):
                if t < NT:
                    if t >= 2:
                        pe.wait_ge(exp_done, t - 1)
                    scores(t)
                if 1 <= t <= NT:
                    turn_p(t - 1)
                if t >= 3 and t % 2 == 1:
                    values((t - 3) // 2)

            def out_proj(i):
                if i < 2:
                    pe.wait_ge(exp_done, NT)
                    pe.wait_ge(pv_cp, 2 * TILES)
                else:
                    pe.wait_ge(mixg, i - 1)
                w0, s0, v0 = item("wo0")
                w1, s1, v1 = item("wo1")
                pe.wait_ge(s0, v0)
                pe.wait_ge(s1, v1)
                for k in range(KC):
                    for hh, w in enumerate((w0, w1)):
                        last = pe.matmul(ps[:, 2 * (i % 2) + hh, :], mix_t[:, k, i * P:(i + 1) * P],
                                         w[:, k * 512:(k + 1) * 512], start=(k == 0), stop=(k == KC - 1))
                last.then_inc(op_mm, 1)

            def turn_use(u):
                if u >= 3:
                    w_ = u - 3
                    i_, part_ = w_ // 4, w_ % 4
                    pe.wait_ge((t2_dve, t2_act, h2_dve, h2_act)[part_], i_ + 1)
                return ps[:, 4 + u % 3, :]

            def second(i):
                pe.wait_ge(xn2_done, i + 1)
                for z in range(2):
                    bank = turn_use(4 * i + z)
                    for k in range(4):
                        kk = 4 * z + k
                        last = transpose(bank[:, k * P:(k + 1) * P], xn2[:, kk * P:(kk + 1) * P])
                    last.then_inc(t2_tr, 1)
                pe.wait_ge(t2_dve, i + 1)
                pe.wait_ge(t2_act, i + 1)
                for z in range(2):
                    bank = turn_use(4 * i + 2 + z)
                    for k in range(4):
                        last = transpose(bank[:, k * P:(k + 1) * P], h2_t[:, i % 2, 4 * z + k, :])
                    last.then_inc(t2_back, 1)
                if i == 0:
                    pe.wait_ge(s_wr, 32)
                else:
                    pe.wait_ge(rt_lg, i)
                for k in range(KC):
                    last = pe.matmul(ps[0:GROUPS + EXPERTS, 7, 0:P], w_r[:, k, :], h2_t[:, i % 2, k, :],
                                     start=(k == 0), stop=(k == KC - 1))
                last.then_inc(rt_mm, 1)
                pe.wait_ge(rt_cp, i + 1)
                transpose(ps[:, 7, P:P + GROUPS + EXPERTS], lg_t[:, :], GROUPS + EXPERTS).then_inc(rt_tr, 1)

            for i in range(TILES + 1):
                if i < TILES:
                    out_proj(i)
                if i:
                    second(i - 1)

            pe.wait_ge(r_both, 1)
            pe.wait_ge(h2_dve, TILES)
            pe.wait_ge(h2_act, TILES)
            for i in range(TILES):
                for m in range(i + 1):
                    pe.matmul(ps[:, 4, i * EXPERTS:(i + 1) * EXPERTS], before_b[:, :] if m == i else ones_b[:, :],
                              both[:, m, :], start=(m == 0), stop=(m == i))
            for m in range(TILES):
                last = pe.matmul(ps[:, 5, 0:EXPERTS], ones_b[:, :], both[:, m, :], start=(m == 0), stop=(m == TILES - 1))
            last.then_inc(r_pos, 1)
            pe.wait_ge(r_sel, 1)
            for m in range(TILES * TOPK):
                last = pe.matmul(ps[:, 6, 0:MAX_TILES], sel_slot[:, m, :], sel_tile[:, m, :],
                                 start=(m == 0), stop=(m == TILES * TOPK - 1))
            last.then_inc(r_idx, 1)

            def turn_x(src, bank, done):
                for cc in range(4):
                    last = transpose(bank[:, cc * P:(cc + 1) * P], src[:, cc * P:(cc + 1) * P])
                last.then_inc(done, 1)

            def gate_up(x_t, w, bank, done):
                gu = w[:, 0:2 * KC * FE].rearrange("p (a k f) -> p a k f", a=2, k=KC)
                for k in range(KC):
                    for fh in range(2):
                        last = pe.matmul(bank[fh * SLOT:(fh + 1) * SLOT, 0:FE].rearrange("p (a f) -> p a f", a=2),
                                         x_t[:, k % 4, (k // 4) * SLOT:(k // 4 + 1) * SLOT],
                                         gu[:, :, k, fh * P:(fh + 1) * P], start=(k == 0), stop=(k == KC - 1))
                last.then_inc(done, 1)

            def down(h, w, bank, done):
                wd = w[:, 2 * KC * FE:3 * KC * FE].rearrange("p (a n) -> p a n", a=2)
                for fh in range(2):
                    for ch in range(2):
                        last = pe.matmul(bank[ch * SLOT:(ch + 1) * SLOT, :], h[:, fh * SLOT:(fh + 1) * SLOT],
                                         wd[:, fh, ch * 512:(ch + 1) * 512], start=(fh == 0), stop=(fh == 1))
                last.then_inc(done, 1)

            def next_x(e, j, it):
                pe.wait_ge(xg_in[j], 16 * (it + 1))
                turn_x(xg[:, j], ps[:, j % 2, :], x_tr)

            def expert(e, j, it, first, last_one):
                w = ring[:, GROUP_OF(j), :]
                pe.wait_ge(ring_in[GROUP_OF(j)], expert_base(GROUP_OF(j)) + 48 * (it + 1))
                pe.wait_ge(x_cp, e + 1)
                if not (first and j < 2):
                    pe.wait_ge(hid_done, e - 1)
                gate_up(xt[:, j % 2], w, ps[:, 2 + j % 2, :], gu2_mm)
                if not (last_one and j == RING - 1):
                    next_x(e + 1, (j + 1) % RING, it + (j + 1) // RING)
                pe.wait_ge(hid_done, e + 1)
                transpose(ps[:, 4 if j % 2 == 0 else 7, 0:P], hid[:, j % 2]).then_inc(ht2_tr, 1)
                pe.wait_ge(ht2_cp, e + 1)
                if not (first and j < 2):
                    pe.wait_ge(y_cp, e - 1)
                down(hid_t[:, j % 2], w, ps[:, 5 + j % 2, :], y_mm)
                lo = pe.value_load(extra_at[0:1, bass.ds(e, 1)], min_val=0, max_val=MAX_EXTRA)
                hi = pe.value_load(extra_at[0:1, bass.ds(e + 1, 1)], min_val=0, max_val=MAX_EXTRA)
                with pe.If(lo < hi), pe.Fori(lo, hi) as x:
                    pe.wait_ge(y_cp, e + 1)
                    pe.wait_ge(e_in, 16 * (x + 1))
                    turn_x(xg_x, ps[:, j % 2, :], e_tr)
                    pe.wait_ge(e_cp, x + 1)
                    gate_up(xt_x, w, ps[:, 2 + j % 2, :], e_gu)
                    pe.wait_ge(e_hid, x + 1)
                    transpose(ps[:, 4 if j % 2 == 0 else 7, 0:P], hid_x[:, :]).then_inc(e_htr, 1)
                    pe.wait_ge(e_htc, x + 1)
                    down(hid_tx, w, ps[:, 5 + j % 2, :], e_y)
                    pe.wait_ge(e_yc, x + 1)
                pe.sem_inc(expert_done, 1)

            pe.wait_ge(r_ready, 1)
            next_x(0, 0, 0)
            NI = EXPERTS // RING
            for j in range(RING):
                expert(j, j, 0, True, False)
            with pe.Fori(1, NI - 1) as it:
                for j in range(RING):
                    expert(it * RING + j, j, it, False, False)
            for j in range(RING):
                expert((NI - 1) * RING + j, j, NI - 1, False, True)

        @block.vector
        def _(dve):
            count = [0]

            def link(ins):
                count[0] += 1
                ins.then_inc(dve_link, 1)
                dve.wait_ge(dve_link, count[0])

            dve.memset(cond[:], 0.0).then_inc(s_zero, 1)
            dve.memset(half_pow[:], -0.5).then_inc(s_zero, 1)
            dve.memset(k_t[:], 0.0)
            link(dve.memset(ones_b[:], 1.0))
            dve.wait_ge(s_const, 32)
            dve.tensor_copy(before_b[:], const("before"))
            dve.tensor_copy(mask_b[:, 0], const("mask_prev"))
            dve.tensor_copy(mask_b[:, 1], const("mask_next"))
            dve.tensor_copy(ident_b[:], ident).then_inc(s_b16, 1)
            dve.wait_ge(s_small, 16)
            dve.tensor_scalar(nsink[:], sink[:], -1.0, None, ALU.mult).then_inc(s_cst2, 1)

            dve.wait_ge(s_colps, 1)
            link(dve.tensor_copy(cols[:], ps[:, 3, 256:256 + N_ROWS]))
            for a in range(KVH):
                last = dve.tensor_copy(k_t[a * HD:(a + 1) * HD, a, 0:P], ps[a * HD:(a + 1) * HD, 3, 128:256])
            last.then_inc(s_cols, 1)

            def row(name, n=KC):
                a, _ = ROWS[name]
                return cols[:, a:a + n]

            dve.wait_ge(s_sq1, TILES)
            dve.tensor_scalar(stats[:, 1, 0:TILES], stats[:, 0, 0:TILES], 1.0 / D, EPS, ALU.mult, ALU.add).then_inc(s_ms1, 1)

            def mod_cols(b):
                dve.wait_ge(mod_mm, b + 1)
                if b >= 2:
                    dve.wait_ge(mod_tr, b - 1)
                dve.tensor_copy(part[:, b % 2].rearrange("p (a f) -> p a f", a=2), ps[:, 0:2, 0:MB // 2]).then_inc(mod_part, 1)

            def mod_sum(b):
                dve.wait_ge(mod_tr, b + 1)
                both_banks = ps[:, 2:4, :].rearrange("p a (j g r) -> p (a j) r g", g=4, r=32)
                j0 = b * MB_CHUNKS
                link(dve.tensor_reduce(mod[:, j0:j0 + MB_CHUNKS, :], both_banks[:, 0:MB_CHUNKS, 0:2, :], AX_X, ALU.add))
                bias = cols[:, ROWS["b_mod"][0] + j0:ROWS["b_mod"][0] + j0 + MB_CHUNKS]
                dve.tensor_tensor(mod[:, j0:j0 + MB_CHUNKS, :], mod[:, j0:j0 + MB_CHUNKS, :],
                                  bias.unsqueeze(2).broadcast_to((P, MB_CHUNKS, 2)), ALU.add).then_inc(mod_col, 1)

            def pre_cols(sub, gain):
                m0 = sub * 3 * KC
                g = row(gain).unsqueeze(2).broadcast_to((P, KC, 2))
                link(dve.tensor_scalar(pre[:, sub, 0], mod[:, m0 + KC:m0 + 2 * KC, :], 1.0, None, ALU.add))
                link(dve.tensor_tensor(pre[:, sub, 0], pre[:, sub, 0], g, ALU.mult))
                link(dve.tensor_copy(pre[:, sub, 1], mod[:, m0:m0 + KC, :]))

            def post_cols(sub, gain):
                m0 = sub * 3 * KC + 2 * KC
                g = row(gain).unsqueeze(2).broadcast_to((P, KC, 2))
                link(dve.tensor_tensor(post[:, sub], mod[:, m0:m0 + KC, :], g, ALU.mult))

            for b in range(3):
                mod_cols(b)
                mod_sum(b)
            dve.wait_ge(mod_col, 3)
            pre_cols(0, "pre_mix")
            dve.engine_nop().then_inc(s_pre1, 1)

            for i in range(TILES):
                dve.wait_ge(ht_tr, i + 1)
                cn = cond_of(i)
                for k in range(4):
                    last = dve.tensor_scalar(h_t[:, k, i * P:(i + 1) * P], ps[:, 4 + 2 * (i % 2), k * P:(k + 1) * P],
                                             pre[:, 0, 0, k, cn:cn + 1], pre[:, 0, 1, k, cn:cn + 1], ALU.mult, ALU.add)
                last.then_inc(ht_dve, 1)

            dve.wait_ge(ht_tr, TILES)
            dve.memset(zeros[:], 0.0).then_inc(s_zero, 1)

            def rotate(i):
                dve.wait_ge(qkv_mm, i + 1)
                if i >= 2:
                    dve.wait_ge(qk_tr, i - 1)
                rot = qk_rot[:, i % 2]

                def pairs(q):
                    return q[:, 0:ATT].rearrange("p (g a d) -> p a g d", a=KVH, d=HD)

                bank = ps[:, 4 + 2 * (i % 2), 0:ATT].rearrange("p (a g d) -> p a g d", a=KVH, d=HD)
                if i == 0:
                    dve.tensor_copy(pairs(rot), bank).then_inc(q_read, 1)
                    dve.wait_ge(kv_read, i + 1)
                    dve.tensor_copy(rot[:, ATT:], k_raw[:, 0]).then_inc(rot_done, 1)
                    return
                dve.wait_ge(rot_done, i)
                cs = const("cos").rearrange("p (t d) -> p t d", t=4)[:, i - 1]
                sn = const("sin").rearrange("p (t d) -> p t d", t=4)[:, i - 1]
                for dst, tab in ((rot, cs), (qk_sin[:, :], sn)):
                    last = dve.tensor_tensor(pairs(dst), bank,
                                             tab.unsqueeze(1).unsqueeze(1).broadcast_to((P, KVH, PAIRS, HD)), ALU.mult)
                last.then_inc(q_read, 1)
                dve.wait_ge(kv_read, i + 1)
                for dst, tab in ((rot, cs), (qk_sin[:, :], sn)):
                    last = dve.tensor_tensor(dst[:, ATT:].rearrange("p (h d) -> p h d", d=HD),
                                             k_raw[:, i % 2].rearrange("p (h d) -> p h d", d=HD),
                                             tab.unsqueeze(1).broadcast_to((P, KVH, HD)), ALU.mult)
                link(last)
                r = rot.rearrange("p (a z c) -> p a z c", z=2, c=16)
                s = qk_sin[:, :].rearrange("p (a z c) -> p a z c", z=2, c=16)
                dve.tensor_tensor(r[:, :, 0], r[:, :, 0], s[:, :, 1], ALU.add)
                dve.tensor_tensor(r[:, :, 1], r[:, :, 1], s[:, :, 0], ALU.add).then_inc(rot_done, 1)

            def keys_out(i):
                dve.wait_ge(qk_tr, i + 1)
                c_at = (5 if i == 0 else i) * P
                for a in range(KVH):
                    last = dve.tensor_copy(k_t[a * HD:(a + 1) * HD, a, c_at:c_at + P], ps[a * HD:(a + 1) * HD, 3, 0:P])
                last.then_inc(qk_dve, 1)

            for i in range(TILES):
                rotate(i)
                if i:
                    keys_out(i - 1)
            mod_cols(3)
            keys_out(TILES - 1)
            mod_sum(3)
            mod_cols(4)
            mod_sum(4)
            for i in range(TILES):
                dve.wait_ge(gsq_done, i + 1)
                dve.tensor_reduce(gm_stats[:, 0, i * GMH:(i + 1) * GMH],
                                  sq[:, i % 2].rearrange("p (h d) -> p h d", d=GMD), AX_X, ALU.add).then_inc(gv_red, 1)
            dve.wait_ge(gv_red, TILES)
            dve.tensor_scalar(gm_stats[:, 1, :], gm_stats[:, 0, :], 1.0 / GMD, EPS, ALU.mult, ALU.add).then_inc(gv_ms, 1)
            for b in range(5, N_MB):
                mod_cols(b)
                mod_sum(b)
            dve.wait_ge(mod_col, N_MB)
            post_cols(0, "post_mix")
            post_cols(1, "post_ffn")
            dve.engine_nop().then_inc(s_post, 1)
            pre_cols(1, "pre_ffn")
            dve.engine_nop().then_inc(s_pre2, 1)
            dve.wait_ge(gv_rs, 1)
            for i in range(TILES):
                dve.tensor_tensor(gm_v[:, i].rearrange("p (h d) -> p h d", d=GMD),
                                  gm_v[:, i].rearrange("p (h d) -> p h d", d=GMD),
                                  gm_stats[:, 2, i * GMH:(i + 1) * GMH].unsqueeze(2).broadcast_to((P, GMH, GMD)),
                                  ALU.mult).then_inc(gv_scaled, 1)
            for sub in range(2):
                dve.wait_ge(gate_mm, sub + 1)
                for cnd in range(2):
                    last = dve.tensor_copy(gate_bc[:, sub, cnd, :].rearrange("p (a n) -> p a n", a=2),
                                           ps[:, 2 * cnd:2 * cnd + 2, :])
                last.then_inc(gate_cp, 1)
            for h in range(GMH):
                dve.wait_ge(gm_mm, h + 1)
                b_at = ROWS["gm_b"][0] + h
                dve.scalar_tensor_tensor(gm_u[:, :, h * GMD:(h + 1) * GMD],
                                         ps[:, 4 + h % 4, 0:TILES * GMD].rearrange("p (t c) -> p t c", t=TILES),
                                         cols[:, b_at:b_at + 1], gm_u[:, :, h * GMD:(h + 1) * GMD],
                                         ALU.add, ALU.mult).then_inc(gm_done, 1)

            NT = TILES * PAIRS
            MX, NM, SA, SUM, ES, DEN, INV = range(7)

            def width(t):
                i = t // PAIRS
                return P * (1 if i == 0 else 3 if i in (1, 4) else 4)

            def row_max(t):
                g = t % PAIRS
                dve.wait_ge(score_mm, t + 1)
                link(dve.tensor_reduce(att_stats[:, MX, t, :], ps[:, 2 * (t % 2):2 * (t % 2) + 2, 0:width(t)], AX_X, ALU.max))
                ns = nsink[:, :].rearrange("p (a g) -> p g a", a=KVH)[:, g]
                dve.scalar_tensor_tensor(att_stats[:, NM, t, :], att_stats[:, MX, t, :], -SCALE, ns,
                                         ALU.mult, ALU.min).then_inc(neg_max, 1)
                dve.wait_ge(neg_max, t + 1)
                dve.tensor_tensor(att_stats[:, SA, t, :], att_stats[:, NM, t, :], ns, ALU.subtract).then_inc(sink_arg, 1)

            def inverse(t):
                dve.wait_ge(exp_done, t + 1)
                link(dve.tensor_tensor(att_stats[:, DEN, t, :], att_stats[:, SUM, t, :], att_stats[:, ES, t, :], ALU.add))
                dve.reciprocal(att_stats[:, INV, t, :], att_stats[:, DEN, t, :]).then_inc(inv_sum, 1)

            def p_out(t):
                dve.wait_ge(pt_tr, 2 * t + 2)
                if t >= 4:
                    dve.wait_ge(pv_mm, t // 2 - 1)
                w = width(t)
                u = 2 * t + 1
                dve.tensor_copy(p_t[:, (t // 2) % 2, 1, 0:w // P, t % 2, :],
                                ps[:, 5 + u % 3, 0:w].rearrange("p (x q) -> p x q", q=P)).then_inc(pt_odd, 1)

            dve.wait_ge(s_cst2, 1)
            for t in range(NT + 1):
                if t < NT:
                    row_max(t)
                if t >= 1:
                    inverse(t - 1)
                if t >= 2:
                    p_out(t - 2)
            p_out(NT - 1)

            def gated(i):
                dve.wait_ge(sq2, i + 1)
                dve.tensor_scalar(stats[:, 3, i:i + 1], stats[:, 2, i:i + 1], 1.0 / D, EPS, ALU.mult, ALU.add).then_inc(ms2, 1)
                dve.wait_ge(rs2, i + 1)
                if i >= 2:
                    dve.wait_ge(res1, i - 1)
                dve.scalar_tensor_tensor(mix_g[:, i % 2].rearrange("p (a n) -> p a n", a=2),
                                         ps[:, 2 * (i % 2):2 * (i % 2) + 2, :], stats[:, 4, i:i + 1],
                                         gate_bc[:, 0, cond_of(i), :].rearrange("p (a n) -> p a n", a=2),
                                         ALU.mult, ALU.mult).then_inc(mixg, 1)
                dve.wait_ge(sq3, i + 1)
                dve.tensor_scalar(stats[:, 6, i:i + 1], stats[:, 5, i:i + 1], 1.0 / D, EPS, ALU.mult, ALU.add).then_inc(ms3, 1)

            def second(i):
                cn = cond_of(i)
                dve.wait_ge(t2_tr, 2 * i + 1)
                if i >= 2:
                    dve.wait_ge(rt_mm, i - 1)
                for k in range(4):
                    last = dve.tensor_scalar(h2_t[:, i % 2, k, :], ps[:, 4 + (4 * i) % 3, k * P:(k + 1) * P],
                                             pre[:, 1, 0, k, cn:cn + 1], pre[:, 1, 1, k, cn:cn + 1], ALU.mult, ALU.add)
                last.then_inc(t2_dve, 1)
                dve.wait_ge(t2_back, 2 * i + 1)
                if i >= 2:
                    dve.wait_ge(h2_out[i % 2], 16 * (i // 2))
                dve.tensor_copy(h2[:, i % 2, 0:512], ps[:, 4 + (4 * i + 2) % 3, :]).then_inc(h2_dve, 1)
                dve.wait_ge(rt_tr, i + 1)
                dve.tensor_copy(logits[:, i, :], ps[:, 7, P:P + GROUPS + EXPERTS]).then_inc(rt_lg, 1)

            for i in range(TILES + 1):
                if i < TILES:
                    gated(i)
                if i:
                    second(i - 1)

            dve.wait_ge(rt_lg, TILES)
            lg_g, lg_e = logits[:, :, 0:GROUPS], logits[:, :, GROUPS:]
            PAD, TOP, TOP2 = range(3)

            def bc(ap, n):
                return ap.unsqueeze(len(ap.shape)).broadcast_to((*ap.shape, n))

            link(dve.memset(r_8[:, PAD], -3e38))
            link(dve.tensor_copy(r_8[:, PAD, :, 0:GROUPS], lg_g))
            for i in range(TILES):
                link(dve.max(r_8[:, TOP, i], r_8[:, PAD, i]))
                last = dve.max_index(r_i8[:, 0, i], r_8[:, TOP, i], r_8[:, PAD, i])
            link(last)
            GI, DIF, EXG, GSUM, GTOP, Z, Z1, W = 0, 1, 2, 4, 5, 6, 7, 8
            flat = lambda n: r_s[:, n].rearrange("p t k -> p (t k)")[:, 0:TILES]
            link(dve.tensor_copy(flat(GI), r_i8[:, 0, :, 0]))
            oh_g = r_e[:, 0:2].rearrange("p a n -> p (a n)")[:, 0:TILES * GROUPS].rearrange("p (t g) -> p t g", g=GROUPS)
            diff = r_e[:, 2:4].rearrange("p a n -> p (a n)")[:, 0:TILES * GROUPS].rearrange("p (t g) -> p t g", g=GROUPS)
            dve.tensor_tensor(oh_g, const("tile")[:, 0:GROUPS].unsqueeze(1).broadcast_to((P, TILES, GROUPS)),
                              bc(flat(GI), GROUPS), ALU.is_equal)
            dve.tensor_tensor(diff, lg_g, bc(r_8[:, TOP, :, 0], GROUPS), ALU.subtract).then_inc(r_sub, 1)
            dve.wait_ge(r_sub, 1)
            prod = r_prod[:, 0:TILES * EXPERTS].rearrange("p (t g e) -> p t g e", t=TILES, g=GROUPS)
            link(dve.tensor_tensor(prod, lg_e.rearrange("p t (g e) -> p t g e", g=GROUPS), bc(oh_g, EPG), ALU.mult))
            link(dve.tensor_reduce(r_8[:, PAD], prod.rearrange("p t g e -> p t e g"), AX_X, ALU.add))
            for i in range(TILES):
                link(dve.max(r_8[:, TOP2, i], r_8[:, PAD, i]))
                last = dve.max_index(r_i8[:, 1, i], r_8[:, TOP2, i], r_8[:, PAD, i])
            link(last)
            dve.tensor_tensor(flat(DIF), r_8[:, TOP2, :, 1], r_8[:, TOP2, :, 0], ALU.subtract).then_inc(r_sub, 1)
            EID, RANK, BASE, QF, REM, TID, ROW, M0, M1 = range(10, 19)
            link(dve.tensor_copy(r_s[:, EID], r_i8[:, 1, :, 0:TOPK]))
            link(dve.scalar_tensor_tensor(r_s[:, EID], bc(flat(GI), TOPK), float(EPG), r_s[:, EID], ALU.mult, ALU.add))
            link(dve.tensor_tensor(one_hot[:].rearrange("p t k e -> p (t k) e"),
                                   const("tile")[:, 0:EXPERTS].unsqueeze(1).broadcast_to((P, TILES * TOPK, EXPERTS)),
                                   bc(r_s[:, EID].rearrange("p t k -> p (t k)"), EXPERTS), ALU.is_equal))
            dve.tensor_tensor(both[:], one_hot[:, :, 0], one_hot[:, :, 1], ALU.add).then_inc(r_both, 1)
            dve.wait_ge(r_exp, 1)
            link(dve.tensor_reduce(flat(GSUM), diff, AX_X, ALU.add))
            link(dve.reciprocal(flat(GTOP), flat(GSUM)))
            dve.wait_ge(r_exp, 2)
            link(dve.tensor_scalar(flat(Z1), flat(Z), 1.0, None, ALU.add))
            link(dve.reciprocal(flat(W), flat(Z1)))
            link(dve.tensor_tensor(w_tok[:, :, 0], flat(W), flat(GTOP), ALU.mult))
            link(dve.tensor_tensor(w_tok[:, :, 1], w_tok[:, :, 0], flat(Z), ALU.mult))
            dve.wait_ge(r_pos, 1)
            pos = ps[:, 4, 0:TILES * EXPERTS].rearrange("p (t e) -> p t e", t=TILES)
            ohp = r_prod[:, 0:TILES * TOPK * EXPERTS].rearrange("p (t k e) -> p t k e", t=TILES, k=TOPK)
            link(dve.tensor_tensor(ohp, one_hot[:], pos.unsqueeze(2).broadcast_to((P, TILES, TOPK, EXPERTS)), ALU.mult))
            link(dve.tensor_reduce(r_s[:, RANK], ohp, AX_X, ALU.add))
            link(dve.tensor_scalar(r_ei[:], ps[:, 5, 0:EXPERTS], 1.0, -1.0, ALU.max, ALU.add))
            link(dve.tensor_scalar(r_ei[:], r_ei[:], 6, None, ALU.arith_shift_right))
            link(dve.tensor_copy(r_e[:, 0, 0:EXPERTS], r_ei[:]))
            dve.memset(r_e[:, 1, :], 0.0)
            link(dve.memset(r_e[:, 2, :], 0.0))
            link(dve.tensor_tensor_scan(r_e[:, 1, 1:EXPERTS + 1], r_e[:, 0, 0:EXPERTS], r_e[:, 2, 0:EXPERTS], 0.0, ALU.add, ALU.add))
            dve.tensor_copy(extra_at[:], r_e[:, 1, :])
            link(dve.tensor_tensor(ohp.rearrange("p t k e -> p (t k) e"), one_hot[:].rearrange("p t k e -> p (t k) e"),
                                   r_e[:, 1, 0:EXPERTS].unsqueeze(1).broadcast_to((P, TILES * TOPK, EXPERTS)), ALU.mult))
            link(dve.tensor_reduce(r_s[:, BASE], ohp, AX_X, ALU.add))
            link(dve.tensor_copy(r_i[:, 0], r_s[:, RANK]))
            dve.tensor_scalar(r_i[:, 1], r_i[:, 0], 6, None, ALU.arith_shift_right)
            link(dve.tensor_scalar(r_i[:, 2], r_i[:, 0], SLOT - 1, None, ALU.bitwise_and))
            dve.tensor_copy(r_s[:, QF], r_i[:, 1])
            link(dve.tensor_copy(r_s[:, REM], r_i[:, 2]))
            link(dve.scalar_tensor_tensor(r_s[:, M0], r_s[:, BASE], float(EXPERTS - 1), r_s[:, QF], ALU.add, ALU.add))
            link(dve.tensor_tensor(r_s[:, M0], r_s[:, M0], r_s[:, EID], ALU.subtract))
            link(dve.tensor_scalar(r_s[:, M1], r_s[:, QF], 0.5, None, ALU.is_gt))
            link(dve.tensor_tensor(r_s[:, M0], r_s[:, M0], r_s[:, M1], ALU.mult))
            link(dve.tensor_tensor(r_s[:, TID], r_s[:, M0], r_s[:, EID], ALU.add))
            link(dve.scalar_tensor_tensor(r_s[:, ROW], r_s[:, TID], float(SLOT), r_s[:, REM], ALU.mult, ALU.add))
            dve.tensor_copy(back_row[:], r_s[:, ROW])
            for i in range(TILES):
                for k in range(TOPK):
                    m = i * TOPK + k
                    dve.tensor_scalar(sel_slot[:, m, :], const("slot"), r_s[:, REM, i, k:k + 1], None, ALU.is_equal)
                    last = dve.tensor_scalar(sel_tile[:, m, :], const("tile"), r_s[:, TID, i, k:k + 1],
                                             const("token")[:, i:i + 1], ALU.is_equal, ALU.mult)
            last.then_inc(r_sel, 1)
            dve.wait_ge(r_idx, 1)
            dve.tensor_scalar(tile_src[:], ps[:, 6, 0:MAX_TILES], const("half"), None, ALU.add).then_inc(r_ready, 1)

            def copy_x(e, j, first):
                dve.wait_ge(x_tr, e + 1)
                if not (first and j < 2):
                    dve.wait_ge(gu2_mm, e - 1)
                dve.tensor_copy(xt[:, j % 2].rearrange("p c s -> p (c s)"), ps[:, j % 2, :]).then_inc(x_cp, 1)

            def expert(e, j, first, last_one):
                if not (last_one and j == RING - 1):
                    copy_x(e + 1, j + 1, first and j == 0)
                dve.wait_ge(silu_done, e + 1)
                if not (first and j < 2):
                    dve.wait_ge(ht2_tr, e - 1)
                dve.tensor_tensor(hid[:, j % 2], act_g[:, j % 2], ps[:, 2 + j % 2, P:2 * P], ALU.mult).then_inc(hid_done, 1)
                lo = dve.value_load(extra_at[0:1, bass.ds(e, 1)], min_val=0, max_val=MAX_EXTRA)
                hi = dve.value_load(extra_at[0:1, bass.ds(e + 1, 1)], min_val=0, max_val=MAX_EXTRA)
                with dve.If(lo < hi), dve.Fori(lo, hi) as x:
                    dve.wait_ge(e_tr, x + 1)
                    dve.tensor_copy(xt_x[:, :, :].rearrange("p c s -> p (c s)"), ps[:, j % 2, :]).then_inc(e_cp, 1)
                    dve.wait_ge(e_silu, x + 1)
                    dve.tensor_tensor(hid_x[:, :], act_x[:, :], ps[:, 2 + j % 2, P:2 * P], ALU.mult).then_inc(e_hid, 1)

            NI = EXPERTS // RING
            dve.wait_ge(r_ready, 1)
            copy_x(0, 0, True)
            for j in range(RING):
                expert(j, j, True, False)
            with dve.Fori(1, NI - 1) as it:
                for j in range(RING):
                    expert(it * RING + j, j, False, False)
            for j in range(RING):
                expert((NI - 1) * RING + j, j, False, True)

            for i in range(TILES):
                dve.wait_ge(back_in[i], 32)
                if i >= 2:
                    dve.wait_ge(f_out, i - 1)
                link(dve.tensor_scalar(y_sum[:, i % 2], y_back[:, i, 0], w_tok[:, i, 0:1], None, ALU.mult))
                dve.scalar_tensor_tensor(y_sum[:, i % 2], y_back[:, i, 1], w_tok[:, i, 1:2], y_sum[:, i % 2],
                                         ALU.mult, ALU.add).then_inc(f_sum, 1)
                dve.wait_ge(f_sq, i + 1)
                dve.tensor_scalar(stats[:, 6, i:i + 1], stats[:, 5, i:i + 1], 1.0 / D, EPS, ALU.mult, ALU.add).then_inc(f_ms, 1)
                dve.wait_ge(f_rs, i + 1)
                if i >= 2:
                    dve.wait_ge(f_st[i % 2], 16 * (i // 2))
                dve.scalar_tensor_tensor(y_sum[:, i % 2], y_sum[:, i % 2], stats[:, 7, i:i + 1],
                                         gate_bc[:, 1, cond_of(i), :], ALU.mult, ALU.mult).then_inc(f_gated, 1)
                dve.wait_ge(f_gated, i + 1)
                dve.tensor_tensor(y_out[:, i % 2], res[:, i], y_sum[:, i % 2], ALU.add).then_inc(f_out, 1)

        @block.scalar
        def _(act):
            act.wait_ge(s_zero, 1)
            act.wait_ge(s_cond, 32)
            act.activation(cond[:, :, 0:2], cond_in[:, :, :], ACT.Silu).then_inc(s_silu, 1)
            for i in range(TILES):
                act.wait_ge(s_xp if i == 0 else s_xs, 16)
                if i:
                    act.wait_ge(s_sq1, i)
                act.activation(junk_1[:], res[:, i], ACT.Square, accum_out=stats[:, 0, i:i + 1]).then_inc(s_sq1, 1)
            act.wait_ge(s_rs1, 1)
            for i in range(TILES):
                act.activation(res[:, i], res[:, i], ACT.Copy, scale=stats[:, 7, i:i + 1]).then_inc(s_xn, 1)
            act.wait_ge(s_pre1, 1)
            for i in range(TILES):
                act.wait_ge(ht_tr, i + 1)
                cn = cond_of(i)
                for k in range(4, KC):
                    last = act.activation(h_t[:, k, i * P:(i + 1) * P], ps[:, 5 + 2 * (i % 2), (k - 4) * P:(k - 3) * P],
                                          ACT.Identity, bias=pre[:, 0, 1, k, cn:cn + 1], scale=pre[:, 0, 0, k, cn:cn + 1])
                last.then_inc(ht_act, 1)

            def queries_out(i):
                act.wait_ge(qk_tr, i + 1)
                act.copy(q_t[:, :, i * P:(i + 1) * P], ps[:, 2, :].rearrange("p (g q) -> p g q", q=P)).then_inc(qk_act, 1)

            for i in range(TILES):
                act.wait_ge(qkv_mm, i + 1)
                if i >= 2:
                    act.wait_ge(rot_done, i - 1)
                if i == 2:
                    act.wait_ge(s_newkv, 16)
                bank = ps[:, 5 + 2 * (i % 2), :]
                act.copy(k_raw[:, i % 2], bank[:, 0:KVW])
                act.copy(v_all[:, 5 if i == 0 else i, :], bank[:, KVW:2 * KVW]).then_inc(kv_read, 1)
                if i == 0:
                    act.wait_ge(kv_read, 1)
                    act.dma_start(new_k[0, 0].rearrange("s h d -> s (h d)"), k_raw[:, 0]).then_inc(s_newkv, 16)
                    act.dma_start(new_v[0, 0].rearrange("s h d -> s (h d)"), v_all[:, 5, :]).then_inc(s_newkv, 16)
                    act.wait_ge(s_newkv, 32)
                else:
                    queries_out(i - 1)
            for u in range(2 * TILES):
                i = u % TILES
                act.wait_ge(gu_mm, u + 1)
                dst = gm_u[:, i] if u < TILES else gm_v[:, i]
                act.activation(dst, ps[:, 4 + u % 4, :], ACT.Gelu_apprx_tanh).then_inc(gelu_done, 1)
                if u == 0:
                    queries_out(TILES - 1)
                if u >= TILES:
                    act.wait_ge(gelu_done, u + 1)
                    if i == 0:
                        act.wait_ge(mod_tr, 5)
                        act.wait_ge(qk_tr, TILES)
                    if i >= 2:
                        act.wait_ge(gv_red, i - 1)
                    act.activation(sq[:, i % 2], gm_v[:, i], ACT.Square).then_inc(gsq_done, 1)
            act.wait_ge(ws_tr, 1)
            act.copy(ws_t[:].rearrange("p (a h) q -> p a (h q)", a=2), ps[:, 0:2, :]).then_inc(ws_cp, 1)
            for i in range(TILES):
                act.wait_ge(gm_tr, i + 1)
                act.copy(mix_t[:, PAIRS:KC, i * P:(i + 1) * P],
                         ps[:, 4 + i % 4, :].rearrange("p (k q) -> p k q", q=P)).then_inc(gm_cp, 1)

            NT = TILES * PAIRS
            MX, NM, SA, SUM, ES, DEN, INV = range(7)

            def width(t):
                i = t // PAIRS
                return P * (1 if i == 0 else 3 if i in (1, 4) else 4)

            def exps(t):
                act.wait_ge(sink_arg, t + 1)
                act.activation(att_stats[:, ES, t, :], att_stats[:, SA, t, :], ACT.Exp)
                if t >= 2:
                    act.wait_ge(pt_tr, 2 * (t - 2) + 2)
                for a in range(KVH):
                    last = act.activation(probs[:, t % 2, a, 0:width(t)], ps[:, 2 * (t % 2) + a, 0:width(t)], ACT.Exp,
                                          bias=att_stats[:, NM, t, a:a + 1], scale=SCALE,
                                          accum_out=att_stats[:, SUM, t, a:a + 1])
                last.then_inc(exp_done, 1)

            def p_out(t):
                act.wait_ge(pt_tr, 2 * t + 1)
                if t >= 4:
                    act.wait_ge(pv_mm, t // 2 - 1)
                w = width(t)
                act.copy(p_t[:, (t // 2) % 2, 0, 0:w // P, t % 2, :],
                         ps[:, 5 + (2 * t) % 3, 0:w].rearrange("p (x q) -> p x q", q=P)).then_inc(pt_even, 1)

            def values_out(m):
                act.wait_ge(pv_mm, m + 1)
                i, g = m // 2, 2 * (m % 2)
                act.copy(mix_t[:, g:g + 2, i * P:(i + 1) * P], ps[:, 4, 0:2 * P].rearrange("p (g q) -> p g q", q=P)).then_inc(pv_cp, 1)

            for t in range(NT + 3):
                if t < NT:
                    exps(t)
                if 1 <= t <= NT:
                    p_out(t - 1)
                if t >= 3 and t % 2 == 1:
                    values_out((t - 3) // 2)

            def norms(i):
                act.wait_ge(op_mm, i + 1)
                if i:
                    act.wait_ge(sq3, i)
                act.activation(junk_2[:].rearrange("p (a n) -> p a n", a=2), ps[:, 2 * (i % 2):2 * (i % 2) + 2, :], ACT.Square,
                               accum_out=stats[:, 2, i:i + 1]).then_inc(sq2, 1)
                act.wait_ge(res1, i + 1)
                act.activation(junk_2[:], res[:, i], ACT.Square, accum_out=stats[:, 5, i:i + 1]).then_inc(sq3, 1)
                act.wait_ge(rs3, i + 1)
                if i:
                    act.wait_ge(t2_tr, 2 * i)
                act.activation(xn2[:], res[:, i], ACT.Copy, scale=stats[:, 7, i:i + 1]).then_inc(xn2_done, 1)

            def second(i):
                cn = cond_of(i)
                act.wait_ge(t2_tr, 2 * i + 2)
                if i >= 2:
                    act.wait_ge(rt_mm, i - 1)
                for k in range(4, KC):
                    last = act.activation(h2_t[:, i % 2, k, :], ps[:, 4 + (4 * i + 1) % 3, (k - 4) * P:(k - 3) * P],
                                          ACT.Identity, bias=pre[:, 1, 1, k, cn:cn + 1], scale=pre[:, 1, 0, k, cn:cn + 1])
                last.then_inc(t2_act, 1)
                act.wait_ge(t2_back, 2 * i + 2)
                if i >= 2:
                    act.wait_ge(h2_out[i % 2], 16 * (i // 2))
                act.copy(h2[:, i % 2, 512:1024], ps[:, 4 + (4 * i + 3) % 3, :]).then_inc(h2_act, 1)
                act.wait_ge(rt_mm, i + 1)
                act.copy(lg_t[:, :], ps[0:GROUPS + EXPERTS, 7, 0:P]).then_inc(rt_cp, 1)
                act.wait_ge(h2_act, i + 1)
                act.wait_ge(h2_dve, i + 1)
                act.dma_start(h2_dram[i * P:(i + 1) * P, :], h2[:, i % 2]).then_inc(h2_out[i % 2], 16)

            act.wait_ge(s_pre2, 1)
            for i in range(TILES + 1):
                if i < TILES:
                    norms(i)
                if i:
                    second(i - 1)
            diff = r_e[:, 2:4].rearrange("p a n -> p (a n)")[:, 0:TILES * GROUPS]
            flat = lambda n: r_s[:, n].rearrange("p t k -> p (t k)")[:, 0:TILES]
            act.wait_ge(r_sub, 1)
            act.activation(diff, diff, ACT.Exp).then_inc(r_exp, 1)
            act.wait_ge(r_sub, 2)
            act.activation(flat(6), flat(1), ACT.Exp).then_inc(r_exp, 1)

            def store_y(src, dst, done):
                for ch in range(2):
                    act.dma_start(dst[:, ch * 512:(ch + 1) * 512], src[ch * SLOT:(ch + 1) * SLOT, :]).then_inc(done, 16)

            def expert(e, j, it, first):
                act.wait_ge(gu2_mm, e + 1)
                if not (first and j < 2):
                    act.wait_ge(hid_done, e - 1)
                act.activation(act_g[:, j % 2], ps[:, 2 + j % 2, 0:P], ACT.Silu).then_inc(silu_done, 1)
                act.wait_ge(ht2_tr, e + 1)
                if not (first and j < 2):
                    act.wait_ge(y_mm, e - 1)
                act.copy(hid_t[:, j % 2], ps[:, 4 if j % 2 == 0 else 7, 0:P]).then_inc(ht2_cp, 1)
                act.wait_ge(y_mm, e + 1)
                if not (first and j < 2):
                    act.wait_ge(y_st[j % 2], 64 * it + 32 * (j // 2))
                act.copy(y_sb[:, j % 2], ps[:, 5 + j % 2, :]).then_inc(y_cp, 1)
                act.wait_ge(y_cp, e + 1)
                store_y(y_sb[:, j % 2], y_dram[e], y_st[j % 2])
                lo = act.value_load(extra_at[0:1, bass.ds(e, 1)], min_val=0, max_val=MAX_EXTRA)
                hi = act.value_load(extra_at[0:1, bass.ds(e + 1, 1)], min_val=0, max_val=MAX_EXTRA)
                with act.If(lo < hi), act.Fori(lo, hi) as x:
                    act.wait_ge(e_gu, x + 1)
                    act.activation(act_x[:, :], ps[:, 2 + j % 2, 0:P], ACT.Silu).then_inc(e_silu, 1)
                    act.wait_ge(e_htr, x + 1)
                    act.copy(hid_tx[:, :], ps[:, 4 if j % 2 == 0 else 7, 0:P]).then_inc(e_htc, 1)
                    act.wait_ge(e_y, x + 1)
                    act.copy(y_x[:, :], ps[:, 5 + j % 2, :]).then_inc(e_yc, 1)
                    act.wait_ge(e_yc, x + 1)
                    store_y(y_x, y_dram[EXPERTS + x], e_st)
                    act.wait_ge(e_st, 32 * (x + 1))

            NI = EXPERTS // RING
            act.wait_ge(r_ready, 1)
            for j in range(RING):
                expert(j, j, 0, True)
            with act.Fori(1, NI) as it:
                for j in range(RING):
                    expert(it * RING + j, j, it, False)
            act.sem_inc(e_all, 1)

            for i in range(TILES):
                act.wait_ge(f_sum, i + 1)
                if i:
                    act.wait_ge(f_sq, i)
                act.activation(junk_3[:], y_sum[:, i % 2], ACT.Square, accum_out=stats[:, 5, i:i + 1]).then_inc(f_sq, 1)
                act.wait_ge(f_out, i + 1)
                dst = y_prompt[0] if i == 0 else y_sample[0, (i - 1) * P:i * P, :]
                act.dma_start(dst, y_out[:, i % 2]).then_inc(f_st[i % 2], 16)
            act.wait_ge(f_st[0], 16 * 3)
            act.wait_ge(f_st[1], 16 * 2)

        @block.gpsimd
        def _(pool):
            pool.dma_start(rows[ROWS["b_mod"][0]:ROWS["b_mod"][1], :],
                           b_mod[0].rearrange("(r q) -> r q", q=P)).then_inc(s_rows, 16)
            for name, src in (("pre_mix", g_pre_mix), ("post_mix", g_post_mix), ("pre_ffn", g_pre_ffn), ("post_ffn", g_post_ffn)):
                pool.dma_start(rows[ROWS[name][0]:ROWS[name][1], :], src[0].rearrange("(r q) -> r q", q=P)).then_inc(s_rows, 16)
            pool.dma_start(rows[ROWS["gm_b"][0]:ROWS["gm_b"][1], :], gm_b[0]).then_inc(s_rows, 16)
            pool.dma_start(cache_sb[:, :], cache_k[0, 0].rearrange("s h d -> s (h d)")).then_inc(s_cache, 16)
            pool.dma_start(v_all[:, 0, :], cache_v[0, 0].rearrange("s h d -> s (h d)")).then_inc(s_cache, 16)
            pool.dma_start(sink[:], attn_sink[0:1, :].broadcast_to((P, HEADS))).then_inc(s_small, 16)
            pool.dma_start(w_r[:, :, 0:GROUPS], router_group[0].rearrange("(k p) f -> p k f", p=P),
                           allow_slow_non_contiguous=True).then_inc(s_wr, 16)
            pool.dma_start(w_r[:, :, GROUPS:], router_expert[0].rearrange("(k p) f -> p k f", p=P)).then_inc(s_wr, 16)

            def rsqrt(dst, src, n, done):
                pool.tensor_tensor(dst, src, half_pow[:, 0:n], ALU.pow).then_inc(done, 1)

            pool.wait_ge(s_zero, 2)
            pool.wait_ge(s_ms1, 1)
            rsqrt(stats[:, 7, 0:TILES], stats[:, 1, 0:TILES], TILES, s_rs1)

            pool.wait_ge(s_zero, 3)
            pool.dma_start(y_dram[EXPERTS:].rearrange("a s (c n) -> (s c) a n", n=512),
                           zeros[:].unsqueeze(1).broadcast_to((P, MAX_EXTRA, 512))).then_inc(s_filled, 16)

            pool.wait_ge(gu_mm, 2 * TILES)
            pool.wait_ge(gv_ms, 1)
            rsqrt(gm_stats[:, 2, :], gm_stats[:, 1, :], TILES * GMH, gv_rs)
            pool.wait_ge(mod_tr, N_MB)
            pool.wait_ge(rot_done, TILES)
            pool.wait_ge(gv_red, TILES)
            pool.dma_start(gmn_bc[:], gm_norm.rearrange("a h d -> a (h d)").broadcast_to((P, GM))).then_inc(s_gmn, 16)
            pool.dma_start(ws_raw[:], gm_ws[0].rearrange("h p q -> p h q")).then_inc(s_ws, 16)
            pool.wait_ge(s_gmn, 16)
            for i in range(TILES):
                pool.wait_ge(gv_scaled, i + 1)
                pool.tensor_tensor(gm_v[:, i], gm_v[:, i], gmn_bc[:], ALU.mult).then_inc(gv_ready, 1)
            pool.wait_ge(gm_mm, GMH)
            pool.wait_ge(s_filled, 16)
            pool.dma_start(res[:, 0, :], x_prompt[0]).then_inc(s_xre, 16)
            pool.dma_start(res[:, 1:TILES, :], x_lat).then_inc(s_xre, 16)

            NT = TILES * PAIRS
            INV = 6
            for t in range(NT):
                i = t // PAIRS
                w = P * (1 if i == 0 else 3 if i in (1, 4) else 4)
                pool.wait_ge(inv_sum, t + 1)
                for a in range(KVH):
                    last = pool.tensor_scalar(probs[:, t % 2, a, 0:w], probs[:, t % 2, a, 0:w],
                                              att_stats[:, INV, t, a:a + 1], None, ALU.mult)
                last.then_inc(p_norm, 1)

            for i in range(TILES):
                pool.wait_ge(ms2, i + 1)
                rsqrt(stats[:, 4, i:i + 1], stats[:, 3, i:i + 1], 1, rs2)
                pool.wait_ge(mixg, i + 1)
                if i == 0:
                    pool.wait_ge(s_xre, 32)
                pool.tensor_tensor(res[:, i], res[:, i], mix_g[:, i % 2], ALU.add).then_inc(res1, 1)
                pool.wait_ge(ms3, i + 1)
                rsqrt(stats[:, 7, i:i + 1], stats[:, 6, i:i + 1], 1, rs3)

            def gather(e, j):
                pool.tensor_copy(idx_col[:, j, 0:1], tile_src[:, bass.ds(e, 1)]).then_inc(idx_cp, 1)
                pool.wait_ge(idx_cp, e + 1)
                pool.sem_inc(idx_seen, 1)
                pool.indirect_dma_start(xg[:, j, :], None, h2_halves,
                                        bass.IndirectOffsetOnAxis(ap=idx_col[:, j, 0:1], axis=0)).then_inc(xg_in[j], 16)

            def extras(e):
                lo = pool.value_load(extra_at[0:1, bass.ds(e, 1)], min_val=0, max_val=MAX_EXTRA)
                hi = pool.value_load(extra_at[0:1, bass.ds(e + 1, 1)], min_val=0, max_val=MAX_EXTRA)
                with pool.If(lo < hi), pool.Fori(lo, hi) as x:
                    pool.tensor_copy(idx_x[:, 0:1], tile_src[:, bass.ds(EXPERTS + x, 1)]).then_inc(e_idx, 1)
                    pool.wait_ge(e_idx, x + 1)
                    pool.sem_inc(idx_seen, 1)
                    pool.indirect_dma_start(xg_x[:, :], None, h2_halves,
                                            bass.IndirectOffsetOnAxis(ap=idx_x[:, 0:1], axis=0)).then_inc(e_in, 16)
                    pool.wait_ge(e_tr, x + 1)

            pool.wait_ge(r_ready, 1)
            pool.wait_ge(h2_out[0], 16 * 3)
            pool.wait_ge(h2_out[1], 16 * 2)
            pool.wait_ge(op_mm, TILES)
            for j in range(RING):
                gather(j, j)
            NI = EXPERTS // RING
            with pool.Fori(0, NI - 1) as it:
                for j in range(RING):
                    e = it * RING + j
                    extras(e)
                    pool.wait_ge(x_tr, e + 1)
                    gather(e + RING, j)
            for j in range(RING):
                extras((NI - 1) * RING + j)

            pool.wait_ge(y_st[0], 32 * EXPERTS // 2)
            pool.wait_ge(y_st[1], 32 * EXPERTS // 2)
            pool.wait_ge(e_all, 1)
            for i in range(TILES):
                for k in range(TOPK):
                    pool.indirect_dma_start(y_back[:, i, k, :], None, y_rows,
                                            bass.IndirectOffsetOnAxis(ap=back_row[:, i, k:k + 1], axis=0)
                                            ).then_inc(back_in[i], 16)
            for i in range(TILES):
                pool.wait_ge(f_ms, i + 1)
                rsqrt(stats[:, 7, i:i + 1], stats[:, 6, i:i + 1], 1, f_rs)


_INS = ['x_prompt', 'x_sample', 'cache_k', 'cache_v', 'c', 'c_ctx', 'w_mod', 'b_mod', 'g_pre_mix', 'w_in',
        'attn_sink', 'gm_norm', 'gm_ws', 'gm_b', 'w_out', 'g_post_mix', 'g_pre_ffn', 'router_group',
        'router_expert', 'w_gate', 'w_up', 'w_down', 'g_post_ffn']
_OUTS = [((1, CTX, D), 'float32'), ((1, LAT, D), 'float32'),
         ((1, 1, CTX, KVH, HD), 'float32'), ((1, 1, CTX, KVH, HD), 'float32')]


def kernel(**inputs):
    import numpy as _np
    import concourse.bacc as _bacc
    from concourse import mybir as _mybir
    from concourse.bass_utils import run_bass_kernel_spmd as _run

    nc = _bacc.Bacc("TRN2", target_bir_lowering=False, num_devices=1)
    arrays, args = {}, []
    for name in _INS + ["consts"]:
        a = constants() if name == "consts" else _np.ascontiguousarray(inputs[name])
        arrays[f"in_{name}_dram"] = a
        args.append(nc.dram_tensor(f"in_{name}_dram", a.shape, _mybir.dt.from_np(a.dtype), kind="ExternalInput").ap())
    for i, (shape, dtype) in enumerate(_OUTS):
        dt = _mybir.dt.from_np(_np.dtype(dtype))
        args.append(nc.dram_tensor(f"out_{i}_dram", shape, dt, kind="ExternalOutput").ap())
    hybrid_dit_step(nc, *args)
    r = _run(nc, [arrays], core_ids=[0])
    return tuple(r.results[0][f"out_{i}_dram"] for i in range(len(_OUTS)))
```

```python
from contextlib import ExitStack

import concourse.bass as bass
from concourse import mybir

ALU = mybir.AluOpType
ACT = mybir.ActivationFunctionType
F32 = mybir.dt.float32
BF16 = mybir.dt.bfloat16
F16 = mybir.dt.float16
I32 = mybir.dt.int32
U32 = mybir.dt.uint32
AX_X = mybir.AxisListType.X

P = 128
D = 1024
KC = D // P
CTX, LAT = 128, 512
TILES = (CTX + LAT) // P
HEADS, KVH, HD = 8, 2, 64
PAIRS = HEADS // KVH
ATT = HEADS * HD
KVW = KVH * HD
QKV = ATT + 2 * KVW
GMH, GMD = 8, 64
GM = GMH * GMD
N_MOD = 6
GROUPS, EPG = 4, 8
EXPERTS = GROUPS * EPG
FE = 256
TOPK = 2
SLOT = 64
MAX_EXTRA = (TOPK * (CTX + LAT) - 1) // SLOT
MAX_TILES = EXPERTS + MAX_EXTRA
TILE_COLS = MAX_TILES + 1
NO_CODE = 2048
EPS = 1e-6
SCALE = HD ** -0.5
NEG = -1e30

RING = 4
SLOT_ELEMS = 3 * KC * FE
WS = 6
XS = 3
LOOPED = (EXPERTS - 2 - WS) // WS
MB = 768
N_MB = N_MOD * D // MB
MB_CHUNKS = MB // P

CONST_COLS = {}
_at = 0
for _name, _n in (("ident", P), ("slot", P), ("tile", TILE_COLS), ("code", TILES * TOPK), ("half", 1), ("half_out", 1),
                  ("cos", 4 * HD), ("sin", 4 * HD), ("before", P), ("mask_prev", P), ("mask_next", P)):
    CONST_COLS[_name] = (_at, _at + _n)
    _at += _n
N_CONST = _at
N_KEPT = CONST_COLS["before"][0]

ROWS = {}
_at = 0
for _name, _n in (("b_mod", N_MOD * KC), ("pre_mix", KC), ("post_mix", KC), ("pre_ffn", KC),
                  ("post_ffn", KC), ("gm_b", GMH)):
    ROWS[_name] = (_at, _at + _n)
    _at += _n
N_ROWS = _at


def constants():
    import numpy as np
    c = np.zeros((P, N_CONST), np.float32)

    def put(name, value):
        a, b = CONST_COLS[name]
        c[:, a:b] = np.asarray(value, np.float32).reshape(P, b - a)

    i = np.arange(P)
    put("ident", np.eye(P))
    put("before", i[:, None] < i[None, :])
    put("mask_prev", np.where(i[None, :] >= i[:, None], 0.0, NEG))
    put("mask_next", np.where(i[None, :] <= i[:, None], 0.0, NEG))
    put("slot", np.broadcast_to(i[None, :] % SLOT, (P, P)))
    put("tile", np.broadcast_to(np.arange(TILE_COLS)[None, :], (P, TILE_COLS)))
    token = i[:, None, None] + P * np.arange(TILES)[None, :, None]
    put("code", TOPK * token + np.arange(TOPK)[None, None, :] - NO_CODE)
    put("half", i // SLOT)
    put("half_out", i // SLOT + 2 * NO_CODE)
    t = np.arange(LAT)
    inv = np.power(np.float32(10000.0), -np.arange(0, 32, 2, dtype=np.float32) / np.float32(32))
    inv = inv.astype(np.float32)
    row = (t // 64).astype(np.float32)[:, None] * inv[None, :]
    col = (t % 64).astype(np.float32)[:, None] * inv[None, :]
    cos = np.concatenate([np.cos(row), np.cos(row), np.cos(col), np.cos(col)], 1)
    sin = np.concatenate([np.sin(row), -np.sin(row), np.sin(col), -np.sin(col)], 1)
    put("cos", cos.reshape(4, P, HD).transpose(1, 0, 2))
    put("sin", sin.reshape(4, P, HD).transpose(1, 0, 2))
    return c


def hybrid_dit_step(
    nc, x_prompt, x_sample, cache_k, cache_v, c, c_ctx, w_mod, b_mod, g_pre_mix, w_in, attn_sink,
    gm_norm, gm_ws, gm_b, w_out, g_post_mix, g_pre_ffn, router_group, router_expert, w_gate, w_up,
    w_down, g_post_ffn, consts, y_prompt, y_sample, new_k, new_v,
):
    with ExitStack() as ctx:
        def sem(name):
            return ctx.enter_context(nc.semaphore(name))

        base = (nc.sbuf_base + 31) // 32 * 32
        at = [base]

        def sb(name, shape, dt, offset=None):
            size = 4 if dt in (F32, I32, U32) else 2
            n = size
            for s in shape[1:]:
                n *= s
            n = (n + 31) // 32 * 32
            if offset is None:
                offset = at[0]
                at[0] += n
            return nc.alloc_sbuf_tensor_at(name, list(shape), dt, offset=offset)

        def region(n):
            o = at[0]
            at[0] += n
            return o

        KB = 1024
        ring = sb("ring", [P, RING, SLOT_ELEMS], F32)
        cst_at = region((4 * N_KEPT + 31) // 32 * 32)
        cst = sb("cst", [P, N_KEPT], F32, cst_at)
        cols = sb("cols", [P, N_ROWS], F32)
        gates_at = region(16 * KB)
        gate_bc = sb("gate_bc", [P, 2, 2, D], F32, gates_at)
        wo_b = sb("wo_b", [P, 4, 512], F32, gates_at + 8 * KB)
        res_at = region(20 * KB)
        res = sb("res", [P, TILES, D], F32, res_at)
        mod = sb("mod", [P, N_MOD * KC, 2], F32)
        pre = sb("pre", [P, 2, 2, KC, 2], F32)
        post = sb("post", [P, 2, KC, 2], F32)
        cond_in = sb("cond_in", [P, KC, 2], F32)
        cond = sb("cond", [P, KC, 32], F32)
        stats = sb("stats", [P, 8, 8], F32)
        gm_stats = sb("gm_stats", [P, 3, TILES * GMH], F32)
        att_stats = sb("att_stats", [P, 8, TILES * PAIRS, 2], F32)
        nsink = sb("nsink", [P, HEADS], F32)
        sink = sb("sink", [P, HEADS], F32)
        half_pow = sb("half_pow", [P, TILES * GMH], F32)
        ident_b = sb("ident_b", [P, P], BF16)
        ones_b = sb("ones_b", [P, P], BF16)
        before_b = sb("before_b", [P, P], BF16)
        mask_b = sb("mask_b", [P, 2, P], BF16)
        w_r = sb("w_r", [P, KC, GROUPS + EXPERTS], F32)
        src_row = sb("src_row", [P, TILE_COLS], U32)
        dst_row = sb("dst_row", [P, TILE_COLS], U32)
        extra_at = sb("extra_at", [P, EXPERTS + 1], I32)
        w_tok = sb("w_tok", [P, TILES, TOPK], F32)
        a0 = region(20 * KB)
        h_t = sb("h_t", [P, KC, TILES * P], F32, a0)
        mix_t = sb("mix_t", [P, KC, TILES * P], F32, a0)
        xg = sb("xg", [P, XS, 512], F32, a0)
        xt = sb("xt", [P, 2, 4, P], F32, a0 + 6 * KB)
        act_g = sb("act_g", [P, 2, P], F32, a0 + 10 * KB)
        hid = sb("hid", [P, 2, P], F32, a0 + 11 * KB)
        hid_t = sb("hid_t", [P, 2, P], F32, a0 + 12 * KB)
        y_sb = sb("y_sb", [P, 2, 512], F32, a0 + 13 * KB)
        act_x = sb("act_x", [P, P], F32, a0 + 17 * KB)
        hid_x = sb("hid_x", [P, P], F32, a0 + 17 * KB + 512)
        hid_tx = sb("hid_tx", [P, P], F32, a0 + 18 * KB)
        idx_in = sb("idx_in", [P, XS, 8], U32, a0 + 19 * KB)
        idx_out = sb("idx_out", [P, WS, 8], U32, a0 + 19 * KB + 128)
        idx_x = sb("idx_x", [P, 8], U32, a0 + 19 * KB + 384)
        idx_xo = sb("idx_xo", [P, 8], U32, a0 + 19 * KB + 416)
        b0 = region(10 * KB)
        cst_once = sb("cst_once", [P, N_CONST - N_KEPT], F32, b0)
        rows = sb("rows", [N_ROWS, P], F32, b0 + 2 * KB)
        gm_u = sb("gm_u", [P, TILES, GM], F32, b0)
        h2 = sb("h2", [P, 2, D], F32, b0)
        c0 = region(10 * KB)
        q_t = sb("q_t", [P, PAIRS, TILES * P], F32, c0)
        h2_t = sb("h2_t", [P, 2, KC, P], F32, c0)
        t0 = region(16 * KB)
        part = sb("part", [P, 2, MB], F32, t0)
        qk_rot = sb("qk_rot", [P, 2, ATT + KVW], F32, t0 + 6 * KB)
        qk_sin = sb("qk_sin", [P, ATT + KVW], F32, t0 + 11 * KB)
        k_raw = sb("k_raw", [P, 2, KVW], F32, t0 + 13 * KB + 512)
        cache_sb = sb("cache_sb", [P, KVW], F32, t0 + 14 * KB + 512)
        junk_1 = sb("junk_1", [P, D], F32, c0)
        sq = sb("sq", [P, 2, GM], F32, t0)
        p_t = sb("p_t", [P, 2, KVH, 4, 2, P], F32, t0)
        mix_g = sb("mix_g", [P, 2, D], F32, t0)
        xn2 = sb("xn2", [P, D], F32, t0 + 8 * KB)
        lg_t = sb("lg_t", [GROUPS + EXPERTS, P], F32, t0 + 12 * KB)
        sel_slot = sb("sel_slot", [P, TILES * TOPK, P], F16, t0 + 13 * KB)
        d0 = region(9 * KB)
        k_t = sb("k_t", [P, KVH, 6 * P], F32, d0)
        v_all = sb("v_all", [P, 6, KVW], F32, d0 + 6 * KB)
        one_hot = sb("one_hot", [P, TILES, TOPK, EXPERTS], F32, d0)
        r_prod = sb("r_prod", [P, TILES * GROUPS * EPG * TOPK], F32, d0 + 1280)
        both = sb("both", [P, TILES, EXPERTS], BF16, d0 + 2560)
        r_s = sb("r_s", [P, 32, TILES, TOPK], F32, d0 + 3 * KB)
        r_8 = sb("r_8", [P, 3, TILES, 8], F32, d0 + 4352)
        r_i8 = sb("r_i8", [P, 2, TILES, 8], U32, d0 + 4864)
        r_e = sb("r_e", [P, 4, EXPERTS + 1], F32, d0 + 5184)
        r_ei = sb("r_ei", [P, EXPERTS], I32, d0 + 5728)
        r_i = sb("r_i", [P, 3, TILES, TOPK], I32, d0 + 5888)
        code_i = sb("code_i", [P, 2, TILE_COLS], I32, d0 + 7904)
        sel_tile = sb("sel_tile", [P, TILES * TOPK, TILE_COLS], F16, d0 + 6016)
        logits = sb("logits", [P, TILES, GROUPS + EXPERTS], F32, d0 + 7104)
        w_5 = sb("w_5", [P, SLOT_ELEMS], F32, b0)
        w_6 = sb("w_6", [P, 2 * KC * FE], F32, b0 + 24 * KB)
        w_6d = sb("w_6d", [P, KC * FE], F32, gates_at)
        xg_x = sb("xg_x", [P, 512], F32, b0 + 40 * KB)
        y_sb2 = sb("y_sb2", [P, 512], F32, b0 + 42 * KB)
        assert CONST_COLS["cos"][0] % 8 == 0 and CONST_COLS["sin"][1] - CONST_COLS["cos"][0] == 512
        y_x = sb("y_x", [P, 512], F32, cst_at + 4 * CONST_COLS["cos"][0])
        assert d0 + 9 * KB == b0 + 45 * KB
        gm_v = sb("gm_v", [P, TILES, GM], F32, res_at)
        ws_raw = sb("ws_raw", [P, GMH, P], F32, res_at + 10 * KB)
        ws_t = sb("ws_t", [P, GMH, P], F32, res_at + 14 * KB)
        gmn_bc = sb("gmn_bc", [P, GM], F32, res_at + 18 * KB)
        probs = sb("probs", [P, 4, 2, 512], F32, res_at)
        ring_at = base
        y_back = sb("y_back", [P, TILES, TOPK, D], F32, ring_at)
        y_sum = sb("y_sum", [P, TILES, D], F32, ring_at + 40 * KB)
        y_out = sb("y_out", [P, TILES, D], F32, ring_at + 60 * KB)
        junk_3 = sb("junk_3", [P, D], F32, ring_at + 80 * KB)
        assert at[0] <= nc.sbuf_usable_end, (at[0], nc.sbuf_usable_end)

        def const(name):
            a, b = CONST_COLS[name]
            return cst[:, a:b] if b <= N_KEPT else cst_once[:, a - N_KEPT:b - N_KEPT]

        ident = const("ident")

        ps = ctx.enter_context(nc.psum_tensor("ps", [P, 8, 512], F32))

        gates_dram = nc.dram_tensor("gates", [2, 2, D], F32, kind="Internal").ap()
        h2_dram = nc.dram_tensor("h2_rows", [TILES * P, D], F32, kind="Internal").ap()
        y_dram = nc.dram_tensor("expert_results", [TILES * P, TOPK, D], F32, kind="Internal").ap()
        h2_halves = h2_dram.rearrange("t (h n) -> (t h) n", h=2)
        y_halves = y_dram.rearrange("t k (h n) -> (t k h) n", h=2)

        s_const, s_rows, s_qkv, s_xp, s_xs, s_small = (sem(n) for n in (
            "const_in", "rows_in", "qkv_late_in", "xp_in", "xs_in", "small_in"))
        s_cache, s_cv, s_wr, s_ws, s_gmn = (sem(n) for n in ("cache_k_in", "cache_v_in", "wr_in", "ws_in", "gmn_in"))
        ring_in = [sem(f"ring_in{i}") for i in range(RING)]
        s_zero, s_b16, s_cst2 = sem("zeroed"), sem("consts_cast"), sem("consts_made")
        dve_link = sem("dve_link")
        s_silu, s_colps, s_cols = sem("cond_silu"), sem("cols_ps"), sem("cols_made")
        s_sq1, s_ms1, s_rs1, s_xn = sem("sq1"), sem("ms1"), sem("rs1"), sem("xn")
        mod_mm, mod_part, mod_tr, mod_col = sem("mod_mm"), sem("mod_part"), sem("mod_tr"), sem("mod_col")
        s_pre1, s_pre2 = sem("pre1_made"), sem("pre2_made")
        ht_tr, ht_dve, ht_act = sem("ht_tr"), sem("ht_dve"), sem("ht_act")
        h_dve, h_act = sem("h_dve"), sem("h_act")
        qkv_mm, q_read, kv_read, rot_done = sem("qkv_mm"), sem("q_read"), sem("kv_read"), sem("rot_done")
        qk_tr, qk_act, qk_dve, s_newkv = sem("qk_tr"), sem("qk_act"), sem("qk_dve"), sem("newkv_out")
        gu_mm, gelu_done, gsq_done, gv_rs, gv_ms = (
            sem("gu_mm"), sem("gelu_done"), sem("gsq_done"), sem("gv_rs"), sem("gv_ms"))
        gv_red, gv_scaled, gv_ready = sem("gv_red"), sem("gv_scaled"), sem("gv_ready")
        ws_tr, ws_cp, gm_mm, gm_done, gm_tr, gm_cp = (
            sem("ws_tr"), sem("ws_cp"), sem("gm_mm"), sem("gm_done"), sem("gm_tr"), sem("gm_cp"))
        s_gate, s_wob = sem("gates_out"), sem("wo_b_in")
        gate_in = [sem("gate_in0"), sem("gate_in1")]
        s_post = sem("post_made")
        score_mm, neg_max, sink_arg, exp_done, p_norm = (
            sem("score_mm"), sem("neg_max"), sem("sink_arg"), sem("exp_done"), sem("p_norm"))
        pt_tr, pt_even, pt_odd, pv_mm, pv_cp = (
            sem("pt_tr"), sem("pt_even"), sem("pt_odd"), sem("pv_mm"), sem("pv_cp"))
        s_xre = sem("x_again")
        op_mm, sq2, ms2, rs2, mixg, res1, sq3, ms3, rs3, xn2_done = (
            sem(n) for n in ("op_mm", "sq2", "ms2", "rs2", "mixg", "res1", "sq3", "ms3", "rs3", "xn2_done"))
        t2_tr, t2_dve, t2_act, t2_back, h2_dve, h2_act = (
            sem(n) for n in ("t2_tr", "t2_dve", "t2_act", "t2_back", "h2_dve", "h2_act"))
        h2_out = [sem("h2_out0"), sem("h2_out1")]
        rt_mm, rt_cp, rt_tr, rt_lg = sem("rt_mm"), sem("rt_cp"), sem("rt_tr"), sem("rt_lg")
        r_sub, r_exp, r_both, r_pos, r_sel, r_idx, r_ready = (
            sem(n) for n in ("r_sub", "r_exp", "r_both", "r_pos", "r_sel", "r_idx", "r_ready"))
        xg_in = [sem(f"xg_in{i}") for i in range(XS)]
        we_in = [sem(f"we_in{k}") for k in range(WS)]
        x_tr, x_cp, gu2_mm, silu_done, hid_done, ht2_tr, ht2_cp, y_mm, y_cp = (
            sem(n) for n in ("x_tr", "x_cp", "gu2_mm", "silu_done", "hid_done", "ht2_tr", "ht2_cp", "y_mm", "y_cp"))
        y_st = [sem(f"y_st{i}") for i in range(XS)]
        expert_done, reload_seen, idx_cp, idx_seen, out_idx = sem("expert_done"), sem("reload_seen"), sem("idx_cp"), sem("idx_seen"), sem("out_idx")
        e_in, e_idx, e_out, e_tr, e_cp, e_gu, e_silu, e_hid, e_htr, e_htc, e_y, e_yc, e_st, e_all, xg_zero = (
            sem("extra_" + n) for n in ("in", "idx", "out", "tr", "cp", "gu", "silu", "hid", "htr", "htc",
                                        "y", "yc", "st", "all", "zero"))
        back_in = [sem(f"back_in{i}") for i in range(TILES)]
        f_first, f_sum, f_sq, f_ms, f_rs, f_out = (
            sem("fin_" + n) for n in ("first", "sum", "sq", "ms", "rs", "out"))
        f_st = sem("fin_st")

        ITEMS = ["m0", "m1", "m2", "qkv", "m3", "gu", "m4", "gv", "m5", "m6", "m7", "wo"]
        N_FIRST = len(ITEMS)
        DMAS = [5 if i == "wo" else 1 for i in ITEMS]
        USED = {f"m{b}": (mod_mm, b + 1) for b in range(N_MB)}
        USED.update({"qkv": (qkv_mm, TILES), "gu": (gu_mm, TILES), "gv": (gu_mm, 2 * TILES),
                     "wo": (op_mm, TILES)})

        def slot_of(r):
            return r % RING

        def landed(r):
            return 16 * sum(DMAS[i] for i in range(r % RING, r + 1, RING))

        def item(name):
            r = ITEMS.index(name)
            return ring[:, slot_of(r), :], ring_in[slot_of(r)], landed(r)

        def weights(c):
            n = 2 * KC * FE
            gu, wd = (w_6[:, :], w_6d[:, :]) if c == 5 else (w_5[:, 0:n], w_5[:, n:]) if c == 4 else (
                ring[:, (N_FIRST + c) % RING, 0:n], ring[:, (N_FIRST + c) % RING, n:])
            return gu.rearrange("p (a k f) -> p a k f", a=2, k=KC), wd.rearrange("p (a n) -> p a n", a=2)

        def y_buf(c):
            return y_sb2[:, :] if c % XS == 2 else y_sb[:, c % XS]

        def nth(q, c, d=0):
            return q + (c + d) // WS, (c + d) % WS

        def below(e, n):
            return isinstance(e, int) and e < n

        def all_experts(engine, step):
            for c in range(2):
                step(0, c)
            with engine.Fori(0, LOOPED) as q:
                for c in range(2, 2 + WS):
                    step(*nth(q, c))
            for e in range(2 + LOOPED * WS, EXPERTS):
                step(*nth(0, e))

        def cond_of(i):
            return 0 if i == 0 else 1

        x_lat = x_sample[0].rearrange("(t p) d -> p t d", p=P)

        block = ctx.enter_context(nc.Block())

        @block.sync
        def _(sp):
            sp.dma_start(cst[:], consts[:, 0:N_KEPT]).then_inc(s_const, 16)
            sp.dma_start(cst_once[:], consts[:, N_KEPT:]).then_inc(s_const, 16)
            sp.dma_start(cond_in[:, :, 0], c_ctx.rearrange("(p k) -> p k", k=KC),
                         allow_slow_non_contiguous=True).then_inc(s_rows, 16)
            sp.dma_start(cond_in[:, :, 1], c[0].rearrange("(p k) -> p k", k=KC),
                         allow_slow_non_contiguous=True).then_inc(s_rows, 16)
            for name, src in (("b_mod", b_mod), ("pre_mix", g_pre_mix), ("post_mix", g_post_mix),
                              ("pre_ffn", g_pre_ffn), ("post_ffn", g_post_ffn)):
                sp.dma_start(rows[ROWS[name][0]:ROWS[name][1], :], src[0].rearrange("(r q) -> r q", q=P)).then_inc(s_rows, 16)
            sp.dma_start(rows[ROWS["gm_b"][0]:ROWS["gm_b"][1], :], gm_b[0]).then_inc(s_rows, 16)
            sp.dma_start(cache_sb[:, :], cache_k[0, 0].rearrange("s h d -> s (h d)")).then_inc(s_cache, 16)
            sp.dma_start(res[:, 0, :], x_prompt[0]).then_inc(s_xp, 16)
            sp.dma_start(res[:, 1:TILES, :], x_lat).then_inc(s_xs, 16)
            for r, name in enumerate(ITEMS):
                if r >= RING:
                    s, v = USED[ITEMS[r - RING]]
                    sp.wait_ge(s, v)
                dst, done = ring[:, slot_of(r), :], ring_in[slot_of(r)]
                if name[0] == "m":
                    b = int(name[1])
                    sp.dma_start(dst.rearrange("p (k f) -> p k f", k=KC),
                                 w_mod[0, :, b * MB:(b + 1) * MB].rearrange("(p k) f -> p k f", k=KC)
                                 ).then_inc(done, 16)
                elif name == "qkv":
                    v = dst.rearrange("p (k f) -> p k f", k=KC)
                    src = w_in[0, :, 0:QKV].rearrange("(k p) f -> p k f", p=P)
                    sp.dma_start(v[:, 0:2], src[:, 0:2]).then_inc(done, 16)
                    sp.dma_start(v[:, 2:KC], src[:, 2:KC]).then_inc(s_qkv, 16)
                elif name in ("gu", "gv"):
                    a, n = {"gu": (QKV, GM), "gv": (QKV + GM, GM)}[name]
                    sp.dma_start(dst[:, 0:KC * n].rearrange("p (k f) -> p k f", k=KC),
                                 w_in[0, :, a:a + n].rearrange("(k p) f -> p k f", p=P)).then_inc(done, 16)
                else:
                    v = dst.rearrange("p (a f) -> p a f", f=512)
                    for hh in range(2):
                        a, k0 = 512 * hh, KC * hh
                        for kv in range(KVH):
                            sp.dma_start(v[kv * HD:(kv + 1) * HD, k0:k0 + PAIRS, :],
                                         w_out[0, kv * PAIRS * HD:(kv + 1) * PAIRS * HD, a:a + 512]
                                         .rearrange("(g d) n -> d g n", d=HD)).then_inc(done, 16)
                        sp.dma_start(v[:, PAIRS:KC, :] if hh == 0 else wo_b[:],
                                     w_out[0, ATT:, a:a + 512].rearrange("(k p) n -> p k n", p=P)
                                     ).then_inc(done if hh == 0 else s_wob, 16)

            def load_expert(q, c):
                e = q * WS + c
                gu, wd = weights(c)
                for a, w in enumerate((w_gate, w_up)):
                    sp.dma_start(gu[:, a].rearrange("p (h k) f -> p h (k f)", h=2),
                                 w[0, e].rearrange("(h p k) f -> p h (k f)", h=2, p=P)).then_inc(we_in[c], 16)
                sp.dma_start(wd, w_down[0, e].rearrange("(k p) f -> p k f", p=P)).then_inc(we_in[c], 16)

            for j in range(RING - 1):
                s, v = USED[ITEMS[N_FIRST + j - RING]]
                sp.wait_ge(s, v)
                load_expert(0, j)
            sp.wait_ge(s_post, 1)
            for sub in range(2):
                for cnd in range(2):
                    sp.dma_start(gates_dram[sub, cnd].rearrange("(k p) -> p k", p=P), post[:, sub, :, cnd],
                                 allow_slow_non_contiguous=True).then_inc(s_gate, 16)
            sp.wait_ge(s_gate, 16 * 4)
            sp.dma_start(gate_bc[:, 0], gates_dram[0:1].broadcast_to((P, 2, D))).then_inc(gate_in[0], 16)
            s, v = USED[ITEMS[N_FIRST - 1]]
            sp.wait_ge(s, v)
            load_expert(0, RING - 1)
            sp.dma_start(gate_bc[:, 1], gates_dram[1:2].broadcast_to((P, 2, D))).then_inc(gate_in[1], 16)
            sp.wait_ge(sq3, TILES)
            sp.wait_ge(t2_back, 2 * TILES)
            sp.wait_ge(h2_out[0], 16 * 3)
            sp.wait_ge(h2_out[1], 16 * 2)
            load_expert(0, 4)
            sp.wait_ge(r_ready, 1)
            sp.wait_ge(xg_in[XS - 1], 16)
            load_expert(0, 5)

            def reload(q, c):
                e = q * WS + c
                sp.wait_ge(y_mm, e - WS + 1)
                sp.wait_ge(expert_done, e - WS + 1)
                q_, c_ = nth(q, c, -2)
                sp.sem_inc(reload_seen, 1)
                sp.wait_ge(we_in[c_], 48 * (q_ + 1))
                load_expert(q, c)

            with sp.Fori(1, EXPERTS // WS) as q:
                for slot in range(WS):
                    reload(q, slot)
            for e in range(EXPERTS // WS * WS, EXPERTS):
                reload(*nth(0, e))
            for i in range(XS):
                sp.wait_ge(y_st[i], 16 * len(range(i, EXPERTS, XS)))
            sp.wait_ge(e_all, 1)
            for i in range(TILES):
                sp.dma_start(y_back[:, i], y_dram[i * P:(i + 1) * P]).then_inc(back_in[i], 16)
            for i in range(TILES):
                sp.wait_ge(f_out, i + 1)
                dst = y_prompt[0] if i == 0 else y_sample[0, (i - 1) * P:i * P, :]
                sp.dma_start(dst, y_out[:, i]).then_inc(f_st, 16)
            sp.wait_ge(f_st, 16 * TILES)

        @block.tensor
        def _(pe):
            def transpose(out, in_, n_in=P):
                return pe.matmul(out, in_, ident[0:n_in, 0:n_in], is_transpose=True, start=True, stop=True)

            pe.wait_ge(s_const, 32)
            pe.wait_ge(s_rows, 128)
            transpose(ps[:, 3, 256:256 + N_ROWS], rows[:, :], N_ROWS)
            pe.wait_ge(s_cache, 16)
            transpose(ps[:, 3, 128:256], cache_sb[:, :]).then_inc(s_colps, 1)
            pe.wait_ge(s_silu, 1)

            def mod_block(b):
                w, s, v = item(f"m{b}")
                w = w.rearrange("p (k f) -> p k f", k=KC)
                pe.wait_ge(s, v)
                if b:
                    pe.wait_ge(mod_part, b)
                for hh in range(2):
                    for k in range(KC):
                        g = k % 4
                        last = pe.matmul(ps[32 * g:32 * g + 32, hh, 0:MB // 2], cond[:, k, :],
                                         w[:, k, hh * (MB // 2):(hh + 1) * (MB // 2)],
                                         start=(k < 4), stop=(k >= 4))
                last.then_inc(mod_mm, 1)

            def mod_turn(b):
                pe.wait_ge(mod_part, b + 1)
                if b:
                    pe.wait_ge(mod_col, b)
                else:
                    pe.wait_ge(s_cols, 1)
                if b == 3:
                    pe.wait_ge(qk_act, TILES)
                    pe.wait_ge(qk_dve, TILES)
                for j in range(MB_CHUNKS):
                    last = transpose(ps[:, 2 + j // 4, (j % 4) * P:(j % 4 + 1) * P],
                                     part[:, b % 2, j * P:(j + 1) * P])
                last.then_inc(mod_tr, 1)

            def turn_tokens(i):
                pe.wait_ge(s_xn, i + 1)
                if i >= 2:
                    pe.wait_ge(ht_dve, i - 1)
                    pe.wait_ge(ht_act, i - 1)
                for k in range(KC):
                    last = transpose(ps[:, 4 + 2 * (i % 2) + k // 4, (k % 4) * P:(k % 4 + 1) * P],
                                     res[:, i, k * P:(k + 1) * P])
                last.then_inc(ht_tr, 1)

            for b, tiles in enumerate(((0, 1, 2), (3, 4), ())):
                mod_block(b)
                mod_turn(b)
                for i in tiles:
                    turn_tokens(i)

            def turn_qk(i):
                pe.wait_ge(rot_done, i + 1)
                if i == 0:
                    pe.wait_ge(mod_col, 3)
                else:
                    pe.wait_ge(qk_act, i)
                    pe.wait_ge(qk_dve, i)
                for g in range(PAIRS):
                    transpose(ps[:, 2, g * P:(g + 1) * P], qk_rot[:, i % 2, g * P:(g + 1) * P])
                transpose(ps[:, 3, 0:P], qk_rot[:, i % 2, ATT:]).then_inc(qk_tr, 1)

            w, s, v = item("qkv")
            w = w.rearrange("p (k f) -> p k f", k=KC)
            pe.wait_ge(s, v)
            for i in range(TILES):
                if i < 2:
                    pe.wait_ge(h_dve, i + 1)
                    pe.wait_ge(h_act, i + 1)
                else:
                    pe.wait_ge(q_read, i - 1)
                    pe.wait_ge(kv_read, i - 1)
                for k in range(KC):
                    if i == 0 and k == 2:
                        pe.wait_ge(s_qkv, 16)
                    h = h_t[:, k, i * P:(i + 1) * P]
                    pe.matmul(ps[:, 4 + 2 * (i % 2), 0:ATT], h, w[:, k, 0:ATT], start=(k == 0), stop=(k == KC - 1))
                    last = pe.matmul(ps[:, 5 + 2 * (i % 2), 0:2 * KVW], h, w[:, k, ATT:QKV],
                                     start=(k == 0), stop=(k == KC - 1))
                last.then_inc(qkv_mm, 1)
                if i:
                    turn_qk(i - 1)

            def gate_proj(u0, name, between):
                w, s, v = item(name)
                w = w[:, 0:KC * GM].rearrange("p (k f) -> p k f", k=KC)
                pe.wait_ge(s, v)
                for i in range(TILES):
                    u = u0 + i
                    if u >= 4:
                        pe.wait_ge(gelu_done, u - 3)
                    else:
                        pe.wait_ge(q_read, TILES)
                        pe.wait_ge(kv_read, TILES)
                    for k in range(KC):
                        last = pe.matmul(ps[:, 4 + u % 4, :], h_t[:, k, i * P:(i + 1) * P], w[:, k, :],
                                         start=(k == 0), stop=(k == KC - 1))
                    last.then_inc(gu_mm, 1)
                    if i == 0:
                        between()

            mod_block(3)
            gate_proj(0, "gu", lambda: turn_qk(TILES - 1))
            mod_turn(3)
            mod_block(4)

            def spatial_weights():
                mod_turn(4)
                pe.wait_ge(s_ws, 16)
                for h in range(GMH):
                    last = transpose(ps[:, h // 4, (h % 4) * P:(h % 4 + 1) * P], ws_raw[:, h, :])
                last.then_inc(ws_tr, 1)

            gate_proj(TILES, "gv", spatial_weights)
            pe.wait_ge(ws_cp, 1)
            for b in range(5, 7):
                mod_block(b)
                mod_turn(b)

            pe.wait_ge(gv_ready, TILES)
            pe.wait_ge(gelu_done, 2 * TILES)
            for h in range(GMH):
                if h >= 4:
                    pe.wait_ge(gm_done, h - 3)
                pe.matmul(ps[:, 4 + h % 4, 0:TILES * GMD].rearrange("p (t c) -> p t c", t=TILES), ws_t[:, h, :],
                          gm_v[:, :, h * GMD:(h + 1) * GMD], start=True, stop=True).then_inc(gm_mm, 1)
            mod_block(7)
            for i in range(TILES):
                pe.wait_ge(gm_done, GMH)
                if i >= 4:
                    pe.wait_ge(gm_cp, i - 3)
                for cc in range(4):
                    last = transpose(ps[:, 4 + i % 4, cc * P:(cc + 1) * P], gm_u[:, i, cc * P:(cc + 1) * P])
                last.then_inc(gm_tr, 1)
            mod_turn(7)

            def chunks(i):
                if i == 0:
                    return [5]
                n = i - 1
                return [0] + [1 + m for m in range(max(n - 1, 0), min(n + 2, 4))]

            def scores(t):
                i, g = t // PAIRS, t % PAIRS
                ch = chunks(i)
                q = q_t[:, g, i * P:(i + 1) * P]
                for a in range(KVH):
                    bank = ps[:, 2 * (t % 2) + a, :]
                    n = P * len(ch)
                    parts = [(0, ch[0], len(ch))] if i <= 1 else [(0, 0, 1), (1, ch[1], len(ch) - 1)]
                    masks = []
                    if i >= 2:
                        masks.append((1, 0))
                    if 1 <= i <= 3:
                        masks.append((len(ch) - 1, 1))
                    for z, (pos, first, cnt) in enumerate(parts):
                        last = pe.matmul(bank[:, pos * P:(pos + cnt) * P], q, k_t[:, a, first * P:(first + cnt) * P],
                                         start=(z == 0), stop=(z == len(parts) - 1 and not masks),
                                         skip_group_check=True)
                    for z, (pos, m) in enumerate(masks):
                        last = pe.matmul(bank[:, pos * P:(pos + 1) * P], ident_b[:, :], mask_b[:, m, :],
                                         start=False, stop=(z == len(masks) - 1), skip_group_check=True)
                last.then_inc(score_mm, 1)

            def turn_p(t):
                i = t // PAIRS
                pe.wait_ge(p_norm, t + 1)
                for a in range(KVH):
                    u = 2 * t + a
                    if u >= 3:
                        pe.wait_ge(pt_odd if (u - 3) % 2 else pt_even, (u - 3) // 2 + 1)
                    for x in range(len(chunks(i))):
                        last = transpose(ps[:, 5 + u % 3, x * P:(x + 1) * P], probs[:, t % 4, a, x * P:(x + 1) * P])
                    last.then_inc(pt_tr, 1)

            def values(m):
                i = m // 2
                ch = chunks(i)
                pe.wait_ge(pt_even, 2 * m + 2)
                pe.wait_ge(pt_odd, 2 * m + 2)
                if m:
                    pe.wait_ge(pv_cp, m)
                for x, cc in enumerate(ch):
                    for a in range(KVH):
                        last = pe.matmul(ps[a * HD:(a + 1) * HD, 4, 0:2 * P], v_all[:, cc, a * HD:(a + 1) * HD],
                                         p_t[:, m % 2, a, x].rearrange("p g q -> p (g q)"),
                                         start=(x == 0), stop=(x == len(ch) - 1))
                last.then_inc(pv_mm, 1)

            NT = TILES * PAIRS

            def out_proj(i, hh):
                if hh == 0:
                    pe.wait_ge(pv_cp, 2 * (i + 1))
                    if i < 2:
                        pe.wait_ge(exp_done, NT - 1 + i)
                    else:
                        pe.wait_ge(mixg, i - 1)
                w, s0, v0 = item("wo")
                pe.wait_ge(s0, v0)
                pe.wait_ge(s_wob, 16)
                for k in range(KC):
                    c_at = (KC * hh + k) * 512
                    rhs = w[:, c_at:c_at + 512] if c_at < SLOT_ELEMS else wo_b[:, k - PAIRS, :]
                    last = pe.matmul(ps[:, 2 * (i % 2) + hh, :], mix_t[:, k, i * P:(i + 1) * P], rhs,
                                     start=(k == 0), stop=(k == KC - 1))
                if hh:
                    last.then_inc(op_mm, 1)

            pe.wait_ge(qk_act, TILES)
            pe.wait_ge(qk_dve, TILES)
            pe.wait_ge(s_b16, 1)
            pe.wait_ge(gm_cp, TILES)
            pe.wait_ge(mod_col, N_MB)
            pe.wait_ge(s_cv, 16)
            for t in range(NT + 3):
                if t < NT:
                    if t >= 2:
                        pe.wait_ge(exp_done, t - 1)
                    scores(t)
                if t == NT + 1:
                    out_proj(0, 0)
                if 2 <= t < NT + 2:
                    turn_p(t - 2)
                if t == NT + 2:
                    out_proj(0, 1)
                if t >= 4 and t % 2 == 0:
                    values((t - 4) // 2)

            def turn_use(u):
                if u >= 3:
                    w_ = u - 3
                    i_, part_ = w_ // 4, w_ % 4
                    pe.wait_ge((t2_dve, t2_act, h2_dve, h2_act)[part_], i_ + 1)
                return ps[:, 4 + u % 3, :]

            def turn_xn(i):
                pe.wait_ge(xn2_done, i + 1)
                for z in range(2):
                    bank = turn_use(4 * i + z)
                    for k in range(4):
                        kk = 4 * z + k
                        last = transpose(bank[:, k * P:(k + 1) * P], xn2[:, kk * P:(kk + 1) * P])
                    last.then_inc(t2_tr, 1)

            def turn_back(i):
                pe.wait_ge(t2_dve, i + 1)
                pe.wait_ge(t2_act, i + 1)
                if i == 0:
                    pe.wait_ge(s_wr, 32)
                else:
                    pe.wait_ge(rt_lg, i)
                for k in range(KC):
                    last = pe.matmul(ps[0:GROUPS + EXPERTS, 7, 0:P], w_r[:, k, :], h2_t[:, i % 2, k, :],
                                     start=(k == 0), stop=(k == KC - 1))
                last.then_inc(rt_mm, 1)
                for z in range(2):
                    bank = turn_use(4 * i + 2 + z)
                    for k in range(4):
                        last = transpose(bank[:, k * P:(k + 1) * P], h2_t[:, i % 2, 4 * z + k, :])
                    last.then_inc(t2_back, 1)

            def turn_logits(i):
                pe.wait_ge(rt_cp, i + 1)
                transpose(ps[:, 7, P:P + GROUPS + EXPERTS], lg_t[:, :], GROUPS + EXPERTS).then_inc(rt_tr, 1)

            for i in range(1, TILES):
                out_proj(i, 0)
                if i >= 2:
                    turn_back(i - 2)
                out_proj(i, 1)
                if i >= 2:
                    turn_logits(i - 2)
                if i:
                    turn_xn(i - 1)
            turn_back(TILES - 2)
            turn_logits(TILES - 2)
            turn_xn(TILES - 1)
            turn_back(TILES - 1)
            turn_logits(TILES - 1)

            pe.wait_ge(r_both, TILES)
            pe.wait_ge(h2_dve, TILES)
            pe.wait_ge(h2_act, TILES)
            for i in range(TILES):
                for m in range(i + 1):
                    pe.matmul(ps[:, 4, i * EXPERTS:(i + 1) * EXPERTS], before_b[:, :] if m == i else ones_b[:, :],
                              both[:, m, :], start=(m == 0), stop=(m == i))
            for m in range(TILES):
                last = pe.matmul(ps[:, 5, 0:EXPERTS], ones_b[:, :], both[:, m, :], start=(m == 0), stop=(m == TILES - 1))
            last.then_inc(r_pos, 1)
            pe.wait_ge(r_sel, 1)
            for m in range(TILES * TOPK):
                last = pe.matmul(ps[:, 6, 0:TILE_COLS], sel_slot[:, m, :], sel_tile[:, m, :],
                                 start=(m == 0), stop=(m == TILES * TOPK - 1))
            last.then_inc(r_idx, 1)

            def turn_x(src, bank, done):
                columns = src.rearrange("p (q k) -> p k q", k=4)
                for cc in range(4):
                    last = transpose(bank[:, cc * P:(cc + 1) * P], columns[:, cc])
                last.then_inc(done, 1)

            def gate_up(x_t, w, bank, done):
                for k in range(KC):
                    for fh in range(2):
                        last = pe.matmul(bank[fh * SLOT:(fh + 1) * SLOT, 0:FE].rearrange("p (a f) -> p a f", a=2),
                                         x_t[:, k % 4, (k // 4) * SLOT:(k // 4 + 1) * SLOT],
                                         w[:, :, k, fh * P:(fh + 1) * P], start=(k == 0), stop=(k == KC - 1))
                last.then_inc(done, 1)

            def down(h, w, bank, done):
                for fh in range(2):
                    for ch in range(2):
                        last = pe.matmul(bank[ch * SLOT:(ch + 1) * SLOT, :], h[:, fh * SLOT:(fh + 1) * SLOT],
                                         w[:, fh, ch * 512:(ch + 1) * 512], start=(fh == 0), stop=(fh == 1))
                last.then_inc(done, 1)

            def next_x(q, c):
                e = q * WS + c
                pe.wait_ge(xg_in[c % XS], 16 * (q * (WS // XS) + c // XS + 1))
                if not below(e, 2):
                    pe.wait_ge(x_cp, e - 1)
                turn_x(xg[:, c % XS], ps[:, c % 2, :], x_tr)

            def products(q, c):
                e = q * WS + c
                pe.wait_ge(we_in[c], 48 * (q + 1))
                pe.wait_ge(x_cp, e + 1)
                if not below(e, 2):
                    pe.wait_ge(hid_done, e - 1)
                gate_up(xt[:, c % 2], weights(c)[0], ps[:, 2 + c % 2, :], gu2_mm)

            def expert(q, c):
                e = q * WS + c
                wgu, wd = weights(c)
                if not isinstance(e, int) or e + 1 < EXPERTS:
                    products(*nth(q, c, 1))
                pe.wait_ge(hid_done, e + 1)
                transpose(ps[:, 4 if c % 2 == 0 else 7, 0:P], hid[:, c % 2]).then_inc(ht2_tr, 1)
                if not isinstance(e, int) or e + 2 < EXPERTS:
                    next_x(*nth(q, c, 2))
                pe.wait_ge(ht2_cp, e + 1)
                if not below(e, 2):
                    pe.wait_ge(y_cp, e - 1)
                down(hid_t[:, c % 2], wd, ps[:, 5 + c % 2, :], y_mm)
                lo = pe.value_load(extra_at[0:1, bass.ds(e, 1)], min_val=0, max_val=MAX_EXTRA)
                hi = pe.value_load(extra_at[0:1, bass.ds(e + 1, 1)], min_val=0, max_val=MAX_EXTRA)
                with pe.If(lo < hi), pe.Fori(lo, hi) as x:
                    pe.wait_ge(e_in, 16 * (x + 1))
                    turn_x(xg_x[:, :], ps[:, (c + 1) % 2, :], e_tr)
                    pe.wait_ge(e_cp, x + 1)
                    gate_up(xt[:, (c + 1) % 2], wgu, ps[:, 2 + c % 2, :], e_gu)
                    pe.wait_ge(e_hid, x + 1)
                    transpose(ps[:, 4 if c % 2 == 0 else 7, 0:P], hid_x[:, :]).then_inc(e_htr, 1)
                    pe.wait_ge(e_htc, x + 1)
                    pe.wait_ge(y_cp, e + 1)
                    down(hid_tx, wd, ps[:, 5 + c % 2, :], e_y)
                    pe.wait_ge(e_yc, x + 1)
                pe.sem_inc(expert_done, 1)

            pe.wait_ge(r_ready, 1)
            next_x(0, 0)
            next_x(0, 1)
            products(0, 0)
            all_experts(pe, expert)

        @block.vector
        def _(dve):
            count = [0]

            def link(ins):
                count[0] += 1
                ins.then_inc(dve_link, 1)
                dve.wait_ge(dve_link, count[0])

            dve.memset(cond[:], 0.0).then_inc(s_zero, 1)
            dve.memset(half_pow[:], -0.5).then_inc(s_zero, 1)
            dve.memset(k_t[:], 0.0)
            link(dve.memset(ones_b[:], 1.0))
            dve.wait_ge(s_const, 32)
            dve.tensor_copy(before_b[:], const("before"))
            dve.tensor_copy(mask_b[:, 0], const("mask_prev"))
            dve.tensor_copy(mask_b[:, 1], const("mask_next"))
            dve.tensor_copy(ident_b[:], ident).then_inc(s_b16, 1)
            dve.wait_ge(s_small, 16)
            dve.tensor_scalar(nsink[:], sink[:], -1.0, None, ALU.mult).then_inc(s_cst2, 1)

            dve.wait_ge(s_colps, 1)
            link(dve.tensor_copy(cols[:], ps[:, 3, 256:256 + N_ROWS]))
            for a in range(KVH):
                last = dve.tensor_copy(k_t[a * HD:(a + 1) * HD, a, 0:P], ps[a * HD:(a + 1) * HD, 3, 128:256])
            last.then_inc(s_cols, 1)

            def row(name, n=KC):
                a, _ = ROWS[name]
                return cols[:, a:a + n]

            dve.wait_ge(s_sq1, TILES)
            dve.tensor_scalar(stats[:, 1, 0:TILES], stats[:, 0, 0:TILES], 1.0 / D, EPS, ALU.mult, ALU.add).then_inc(s_ms1, 1)

            def mod_cols(b):
                dve.wait_ge(mod_mm, b + 1)
                if b >= 2:
                    dve.wait_ge(mod_tr, b - 1)
                dve.tensor_copy(part[:, b % 2].rearrange("p (a f) -> p a f", a=2), ps[:, 0:2, 0:MB // 2]).then_inc(mod_part, 1)

            def mod_sum(b):
                dve.wait_ge(mod_tr, b + 1)
                both_banks = ps[:, 2:4, :].rearrange("p a (j g r) -> p (a j) r g", g=4, r=32)
                j0 = b * MB_CHUNKS
                link(dve.tensor_reduce(mod[:, j0:j0 + MB_CHUNKS, :], both_banks[:, 0:MB_CHUNKS, 0:2, :], AX_X, ALU.add))
                bias = cols[:, ROWS["b_mod"][0] + j0:ROWS["b_mod"][0] + j0 + MB_CHUNKS]
                dve.tensor_tensor(mod[:, j0:j0 + MB_CHUNKS, :], mod[:, j0:j0 + MB_CHUNKS, :],
                                  bias.unsqueeze(2).broadcast_to((P, MB_CHUNKS, 2)), ALU.add).then_inc(mod_col, 1)

            def pre_cols(sub, gain):
                m0 = sub * 3 * KC
                g = row(gain).unsqueeze(2).broadcast_to((P, KC, 2))
                link(dve.tensor_scalar(pre[:, sub, 0], mod[:, m0 + KC:m0 + 2 * KC, :], 1.0, None, ALU.add))
                link(dve.tensor_tensor(pre[:, sub, 0], pre[:, sub, 0], g, ALU.mult))
                link(dve.tensor_copy(pre[:, sub, 1], mod[:, m0:m0 + KC, :]))

            def post_cols(sub, gain):
                m0 = sub * 3 * KC + 2 * KC
                g = row(gain).unsqueeze(2).broadcast_to((P, KC, 2))
                link(dve.tensor_tensor(post[:, sub], mod[:, m0:m0 + KC, :], g, ALU.mult))

            def tokens_out(i):
                dve.wait_ge(ht_tr, i + 1)
                dve.tensor_copy(h_t[:, 0:4, i * P:(i + 1) * P],
                                ps[:, 4 + 2 * (i % 2), :].rearrange("p (k q) -> p k q", q=P)).then_inc(ht_dve, 1)

            for b, tiles in enumerate(((0, 1, 2), (3, 4), ())):
                mod_cols(b)
                mod_sum(b)
                for i in tiles:
                    tokens_out(i)
            dve.wait_ge(mod_col, 3)
            pre_cols(0, "pre_mix")
            dve.engine_nop().then_inc(s_pre1, 1)
            dve.wait_ge(ht_dve, TILES)
            dve.wait_ge(ht_act, TILES)
            for cn, (a, b) in enumerate(((0, P), (P, TILES * P))):
                for k in range(5):
                    last = dve.tensor_scalar(h_t[:, k, a:b], h_t[:, k, a:b], pre[:, 0, 0, k, cn:cn + 1],
                                             pre[:, 0, 1, k, cn:cn + 1], ALU.mult, ALU.add)
                last.then_inc(h_dve, 1)

            def rotate(i):
                dve.wait_ge(qkv_mm, i + 1)
                if i >= 2:
                    dve.wait_ge(qk_tr, i - 1)
                rot = qk_rot[:, i % 2]

                def pairs(q):
                    return q[:, 0:ATT].rearrange("p (g a d) -> p a g d", a=KVH, d=HD)

                bank = ps[:, 4 + 2 * (i % 2), 0:ATT].rearrange("p (a g d) -> p a g d", a=KVH, d=HD)
                if i == 0:
                    dve.tensor_copy(pairs(rot), bank).then_inc(q_read, 1)
                    dve.wait_ge(kv_read, i + 1)
                    dve.tensor_copy(rot[:, ATT:], k_raw[:, 0]).then_inc(rot_done, 1)
                    return
                dve.wait_ge(rot_done, i)
                cs = const("cos").rearrange("p (t d) -> p t d", t=4)[:, i - 1]
                sn = const("sin").rearrange("p (t d) -> p t d", t=4)[:, i - 1]
                for dst, tab in ((rot, cs), (qk_sin[:, :], sn)):
                    last = dve.tensor_tensor(pairs(dst), bank,
                                             tab.unsqueeze(1).unsqueeze(1).broadcast_to((P, KVH, PAIRS, HD)), ALU.mult)
                last.then_inc(q_read, 1)
                dve.wait_ge(kv_read, i + 1)
                for dst, tab in ((rot, cs), (qk_sin[:, :], sn)):
                    last = dve.tensor_tensor(dst[:, ATT:].rearrange("p (h d) -> p h d", d=HD),
                                             k_raw[:, i % 2].rearrange("p (h d) -> p h d", d=HD),
                                             tab.unsqueeze(1).broadcast_to((P, KVH, HD)), ALU.mult)
                link(last)
                r = rot.rearrange("p (a z c) -> p a z c", z=2, c=16)
                s = qk_sin[:, :].rearrange("p (a z c) -> p a z c", z=2, c=16)
                dve.tensor_tensor(r[:, :, 0], r[:, :, 0], s[:, :, 1], ALU.add)
                dve.tensor_tensor(r[:, :, 1], r[:, :, 1], s[:, :, 0], ALU.add).then_inc(rot_done, 1)

            def keys_out(i):
                dve.wait_ge(qk_tr, i + 1)
                c_at = (5 if i == 0 else i) * P
                for a in range(KVH):
                    last = dve.tensor_copy(k_t[a * HD:(a + 1) * HD, a, c_at:c_at + P], ps[a * HD:(a + 1) * HD, 3, 0:P])
                last.then_inc(qk_dve, 1)

            for i in range(TILES):
                rotate(i)
                if i:
                    keys_out(i - 1)
            mod_cols(3)
            keys_out(TILES - 1)
            mod_sum(3)
            mod_cols(4)
            mod_sum(4)
            def normed_values(i):
                dve.wait_ge(gv_rs, i + 1)
                dve.tensor_tensor(gm_v[:, i].rearrange("p (h d) -> p h d", d=GMD),
                                  gm_v[:, i].rearrange("p (h d) -> p h d", d=GMD),
                                  gm_stats[:, 2, i * GMH:(i + 1) * GMH].unsqueeze(2).broadcast_to((P, GMH, GMD)),
                                  ALU.mult).then_inc(gv_scaled, 1)

            for i in range(TILES):
                heads = slice(i * GMH, (i + 1) * GMH)
                dve.wait_ge(gsq_done, i + 1)
                dve.tensor_reduce(gm_stats[:, 0, heads],
                                  sq[:, i % 2].rearrange("p (h d) -> p h d", d=GMD), AX_X, ALU.add).then_inc(gv_red, 1)
                dve.wait_ge(gv_red, i + 1)
                dve.tensor_scalar(gm_stats[:, 1, heads], gm_stats[:, 0, heads], 1.0 / GMD, EPS, ALU.mult, ALU.add).then_inc(gv_ms, 1)
                if i:
                    normed_values(i - 1)
            mod_cols(5)
            normed_values(TILES - 1)
            mod_sum(5)
            mod_cols(6)
            mod_sum(6)
            for h in range(GMH):
                dve.wait_ge(gm_mm, h + 1)
                b_at = ROWS["gm_b"][0] + h
                dve.scalar_tensor_tensor(gm_u[:, :, h * GMD:(h + 1) * GMD],
                                         ps[:, 4 + h % 4, 0:TILES * GMD].rearrange("p (t c) -> p t c", t=TILES),
                                         cols[:, b_at:b_at + 1], gm_u[:, :, h * GMD:(h + 1) * GMD],
                                         ALU.add, ALU.mult).then_inc(gm_done, 1)
            mod_cols(7)
            mod_sum(7)
            dve.wait_ge(mod_col, N_MB)
            post_cols(0, "post_mix")
            post_cols(1, "post_ffn")
            dve.engine_nop().then_inc(s_post, 1)
            pre_cols(1, "pre_ffn")
            dve.engine_nop().then_inc(s_pre2, 1)
            NT = TILES * PAIRS
            MX, NM, SA, SUM, ES, DEN, INV = range(7)

            def width(t):
                i = t // PAIRS
                return P * (1 if i == 0 else 3 if i in (1, 4) else 4)

            def row_max(t):
                g = t % PAIRS
                dve.wait_ge(score_mm, t + 1)
                link(dve.tensor_reduce(att_stats[:, MX, t, :], ps[:, 2 * (t % 2):2 * (t % 2) + 2, 0:width(t)], AX_X, ALU.max))
                ns = nsink[:, :].rearrange("p (a g) -> p g a", a=KVH)[:, g]
                dve.scalar_tensor_tensor(att_stats[:, NM, t, :], att_stats[:, MX, t, :], -SCALE, ns,
                                         ALU.mult, ALU.min).then_inc(neg_max, 1)
                dve.wait_ge(neg_max, t + 1)
                dve.tensor_tensor(att_stats[:, SA, t, :], att_stats[:, NM, t, :], ns, ALU.subtract).then_inc(sink_arg, 1)

            def normalise(t):
                dve.wait_ge(exp_done, t + 1)
                link(dve.tensor_tensor(att_stats[:, DEN, t, :], att_stats[:, SUM, t, :], att_stats[:, ES, t, :], ALU.add))
                link(dve.reciprocal(att_stats[:, INV, t, :], att_stats[:, DEN, t, :]))
                for a in range(KVH):
                    p = probs[:, t % 4, a, 0:width(t)]
                    last = dve.tensor_scalar(p, p, att_stats[:, INV, t, a:a + 1], None, ALU.mult)
                last.then_inc(p_norm, 1)

            def p_out(t):
                dve.wait_ge(pt_tr, 2 * t + 2)
                if t >= 4:
                    dve.wait_ge(pv_mm, t // 2 - 1)
                w = width(t)
                u = 2 * t + 1
                dve.tensor_copy(p_t[:, (t // 2) % 2, 1, 0:w // P, t % 2, :],
                                ps[:, 5 + u % 3, 0:w].rearrange("p (x q) -> p x q", q=P)).then_inc(pt_odd, 1)

            dve.wait_ge(s_cst2, 1)
            for t in range(NT + 1):
                if t < NT:
                    row_max(t)
                if t >= 1:
                    normalise(t - 1)
                if t >= 2:
                    p_out(t - 2)
            p_out(NT - 1)

            def gated(i):
                dve.wait_ge(sq2, i + 1)
                dve.tensor_scalar(stats[:, 3, i:i + 1], stats[:, 2, i:i + 1], 1.0 / D, EPS, ALU.mult, ALU.add).then_inc(ms2, 1)
                dve.wait_ge(rs2, i + 1)
                if i == 0:
                    dve.wait_ge(gate_in[0], 16)
                dve.scalar_tensor_tensor(mix_g[:, i % 2].rearrange("p (a n) -> p a n", a=2),
                                         ps[:, 2 * (i % 2):2 * (i % 2) + 2, :], stats[:, 4, i:i + 1],
                                         gate_bc[:, 0, cond_of(i), :].rearrange("p (a n) -> p a n", a=2),
                                         ALU.mult, ALU.mult).then_inc(mixg, 1)
                dve.wait_ge(mixg, i + 1)
                if i == 0:
                    dve.wait_ge(s_xre, 32)
                dve.tensor_tensor(res[:, i], res[:, i], mix_g[:, i % 2], ALU.add).then_inc(res1, 1)
                dve.wait_ge(sq3, i + 1)
                dve.tensor_scalar(stats[:, 6, i:i + 1], stats[:, 5, i:i + 1], 1.0 / D, EPS, ALU.mult, ALU.add).then_inc(ms3, 1)

            def scale_h2(i):
                cn = cond_of(i)
                dve.wait_ge(t2_tr, 2 * i + 1)
                if i >= 2:
                    dve.wait_ge(t2_back, 2 * i - 2)
                for k in range(4):
                    last = dve.tensor_scalar(h2_t[:, i % 2, k, :], ps[:, 4 + (4 * i) % 3, k * P:(k + 1) * P],
                                             pre[:, 1, 0, k, cn:cn + 1], pre[:, 1, 1, k, cn:cn + 1], ALU.mult, ALU.add)
                last.then_inc(t2_dve, 1)

            def h2_back(i):
                dve.wait_ge(t2_back, 2 * i + 1)
                if i >= 2:
                    dve.wait_ge(h2_out[i % 2], 16 * (i // 2))
                dve.tensor_copy(h2[:, i % 2, 0:512], ps[:, 4 + (4 * i + 2) % 3, :]).then_inc(h2_dve, 1)
                dve.wait_ge(rt_tr, i + 1)
                dve.tensor_copy(logits[:, i, :], ps[:, 7, P:P + GROUPS + EXPERTS]).then_inc(rt_lg, 1)

            PAD, TOP, TOP2 = range(3)
            GI, DIF, EXG, GSUM, GTOP, Z, Z1, W = 0, 1, 2, 4, 5, 6, 7, 8
            EID, RANK, BASE, QF, REM, TID, M0, M1 = range(10, 18)

            def bc(ap, n):
                return ap.unsqueeze(len(ap.shape)).broadcast_to((*ap.shape, n))

            def flat(n):
                return r_s[:, n].rearrange("p t k -> p (t k)")[:, 0:TILES]

            oh_g = r_e[:, 0:2].rearrange("p a n -> p (a n)")[:, 0:TILES * GROUPS].rearrange("p (t g) -> p t g", g=GROUPS)
            diff = r_e[:, 2:4].rearrange("p a n -> p (a n)")[:, 0:TILES * GROUPS].rearrange("p (t g) -> p t g", g=GROUPS)

            def route(i):
                dve.wait_ge(rt_lg, i + 1)
                lg_g, lg_e = logits[:, i, 0:GROUPS], logits[:, i, GROUPS:]
                link(dve.tensor_copy(r_8[:, PAD, i, 0:GROUPS], lg_g))
                link(dve.max(r_8[:, TOP, i], r_8[:, PAD, i]))
                link(dve.max_index(r_i8[:, 0, i], r_8[:, TOP, i], r_8[:, PAD, i]))
                link(dve.tensor_copy(flat(GI)[:, i:i + 1], r_i8[:, 0, i, 0:1]))
                dve.tensor_scalar(diff[:, i], lg_g, r_8[:, TOP, i, 0:1], None, ALU.subtract).then_inc(r_sub, 1)
                link(dve.tensor_scalar(oh_g[:, i], const("tile")[:, 0:GROUPS], flat(GI)[:, i:i + 1], None, ALU.is_equal))
                prod = r_prod[:, 0:EXPERTS].rearrange("p (g e) -> p g e", g=GROUPS)
                link(dve.tensor_tensor(prod, lg_e.rearrange("p (g e) -> p g e", g=GROUPS), bc(oh_g[:, i], EPG), ALU.mult))
                link(dve.tensor_reduce(r_8[:, PAD, i], prod.rearrange("p g e -> p e g"), AX_X, ALU.add))
                link(dve.max(r_8[:, TOP2, i], r_8[:, PAD, i]))
                link(dve.max_index(r_i8[:, 1, i], r_8[:, TOP2, i], r_8[:, PAD, i]))
                dve.tensor_tensor(flat(DIF)[:, i:i + 1], r_8[:, TOP2, i, 1:2], r_8[:, TOP2, i, 0:1], ALU.subtract).then_inc(r_sub, 1)
                link(dve.tensor_copy(r_s[:, EID, i], r_i8[:, 1, i, 0:TOPK]))
                link(dve.scalar_tensor_tensor(r_s[:, EID, i], bc(flat(GI)[:, i], TOPK), float(EPG), r_s[:, EID, i], ALU.mult, ALU.add))
                link(dve.tensor_tensor(one_hot[:, i], const("tile")[:, 0:EXPERTS].unsqueeze(1).broadcast_to((P, TOPK, EXPERTS)),
                                       bc(r_s[:, EID, i], EXPERTS), ALU.is_equal))
                dve.tensor_tensor(both[:, i], one_hot[:, i, 0], one_hot[:, i, 1], ALU.add).then_inc(r_both, 1)

            for i in range(TILES):
                if i >= 2:
                    h2_back(i - 2)
                if i:
                    scale_h2(i - 1)
                gated(i)
                if i == 1:
                    link(dve.memset(r_8[:, PAD], -3e38))
                if i >= 2:
                    route(i - 2)
            h2_back(TILES - 2)
            scale_h2(TILES - 1)
            route(TILES - 2)
            h2_back(TILES - 1)
            route(TILES - 1)

            dve.wait_ge(r_pos, 1)
            pos = ps[:, 4, 0:TILES * EXPERTS].rearrange("p (t e) -> p t e", t=TILES)
            ohp = r_prod[:, 0:TILES * TOPK * EXPERTS].rearrange("p (t k e) -> p t k e", t=TILES, k=TOPK)
            link(dve.tensor_tensor(ohp, one_hot[:], pos.unsqueeze(2).broadcast_to((P, TILES, TOPK, EXPERTS)), ALU.mult))
            link(dve.tensor_reduce(r_s[:, RANK], ohp, AX_X, ALU.add))
            link(dve.tensor_copy(r_i[:, 0], r_s[:, RANK]))
            dve.tensor_scalar(r_i[:, 1], r_i[:, 0], 6, None, ALU.arith_shift_right)
            link(dve.tensor_scalar(r_i[:, 2], r_i[:, 0], SLOT - 1, None, ALU.bitwise_and))
            dve.tensor_copy(r_s[:, QF], r_i[:, 1])
            link(dve.tensor_copy(r_s[:, REM], r_i[:, 2]))
            dve.tensor_tensor(sel_slot[:], const("slot").unsqueeze(1).broadcast_to((P, TILES * TOPK, P)),
                              bc(r_s[:, REM].rearrange("p t k -> p (t k)"), P), ALU.is_equal)
            link(dve.tensor_scalar(r_ei[:], ps[:, 5, 0:EXPERTS], 1.0, -1.0, ALU.max, ALU.add))
            link(dve.tensor_scalar(r_ei[:], r_ei[:], 6, None, ALU.arith_shift_right))
            dve.wait_ge(r_exp, 1)
            link(dve.tensor_reduce(flat(GSUM), diff, AX_X, ALU.add))
            link(dve.tensor_copy(r_e[:, 0, 0:EXPERTS], r_ei[:]))
            dve.memset(r_e[:, 1, :], 0.0)
            link(dve.memset(r_e[:, 2, :], 0.0))
            link(dve.tensor_tensor_scan(r_e[:, 1, 1:EXPERTS + 1], r_e[:, 0, 0:EXPERTS], r_e[:, 2, 0:EXPERTS], 0.0, ALU.add, ALU.add))
            dve.tensor_copy(extra_at[:], r_e[:, 1, :])
            link(dve.tensor_tensor(ohp.rearrange("p t k e -> p (t k) e"), one_hot[:].rearrange("p t k e -> p (t k) e"),
                                   r_e[:, 1, 0:EXPERTS].unsqueeze(1).broadcast_to((P, TILES * TOPK, EXPERTS)), ALU.mult))
            link(dve.tensor_reduce(r_s[:, BASE], ohp, AX_X, ALU.add))
            link(dve.scalar_tensor_tensor(r_s[:, M0], r_s[:, BASE], float(EXPERTS - 1), r_s[:, QF], ALU.add, ALU.add))
            link(dve.tensor_tensor(r_s[:, M0], r_s[:, M0], r_s[:, EID], ALU.subtract))
            link(dve.tensor_scalar(r_s[:, M1], r_s[:, QF], 0.5, None, ALU.is_gt))
            link(dve.tensor_tensor(r_s[:, M0], r_s[:, M0], r_s[:, M1], ALU.mult))
            link(dve.tensor_tensor(r_s[:, TID], r_s[:, M0], r_s[:, EID], ALU.add))
            link(dve.tensor_tensor(sel_tile[:], const("tile").unsqueeze(1).broadcast_to((P, TILES * TOPK, TILE_COLS)),
                                   bc(r_s[:, TID].rearrange("p t k -> p (t k)"), TILE_COLS), ALU.is_equal))
            dve.tensor_tensor(sel_tile[:], sel_tile[:], bc(const("code"), TILE_COLS), ALU.mult).then_inc(r_sel, 1)
            link(dve.reciprocal(flat(GTOP), flat(GSUM)))
            dve.wait_ge(r_exp, 2)
            link(dve.tensor_scalar(flat(Z1), flat(Z), 1.0, None, ALU.add))
            link(dve.reciprocal(flat(W), flat(Z1)))
            link(dve.tensor_tensor(w_tok[:, :, 0], flat(W), flat(GTOP), ALU.mult))
            link(dve.tensor_tensor(w_tok[:, :, 1], w_tok[:, :, 0], flat(Z), ALU.mult))
            dve.wait_ge(r_idx, 1)
            code = ps[:, 6, 0:TILE_COLS]
            dve.tensor_scalar(dst_row[:], code, 2.0, const("half_out"), ALU.mult, ALU.add)
            link(dve.tensor_scalar(code_i[:, 0], code, float(NO_CODE), None, ALU.add))
            link(dve.tensor_scalar(code_i[:, 1], code_i[:, 0], 1, None, ALU.arith_shift_right))
            dve.tensor_scalar(src_row[:], code_i[:, 1], 2.0, const("half"), ALU.mult, ALU.add).then_inc(r_ready, 1)

            def copy_x(q, c):
                e = q * WS + c
                dve.wait_ge(x_tr, e + 1)
                if not below(e, 2):
                    dve.wait_ge(gu2_mm, e - 1)
                dve.tensor_copy(xt[:, c % 2].rearrange("p c s -> p (c s)"), ps[:, c % 2, :]).then_inc(x_cp, 1)

            def hidden(q, c):
                e = q * WS + c
                dve.wait_ge(silu_done, e + 1)
                if not below(e, 2):
                    dve.wait_ge(ht2_tr, e - 1)
                dve.tensor_tensor(hid[:, c % 2], act_g[:, c % 2], ps[:, 2 + c % 2, P:2 * P], ALU.mult).then_inc(hid_done, 1)

            def expert(q, c):
                e = q * WS + c
                if not isinstance(e, int) or e + 1 < EXPERTS:
                    hidden(*nth(q, c, 1))
                if not isinstance(e, int) or e + 2 < EXPERTS:
                    copy_x(*nth(q, c, 2))
                lo = dve.value_load(extra_at[0:1, bass.ds(e, 1)], min_val=0, max_val=MAX_EXTRA)
                hi = dve.value_load(extra_at[0:1, bass.ds(e + 1, 1)], min_val=0, max_val=MAX_EXTRA)
                with dve.If(lo < hi), dve.Fori(lo, hi) as x:
                    dve.wait_ge(e_tr, x + 1)
                    dve.tensor_copy(xt[:, (c + 1) % 2].rearrange("p c s -> p (c s)"), ps[:, (c + 1) % 2, :]).then_inc(e_cp, 1)
                    dve.wait_ge(e_silu, x + 1)
                    dve.tensor_tensor(hid_x[:, :], act_x[:, :], ps[:, 2 + c % 2, P:2 * P], ALU.mult).then_inc(e_hid, 1)

            dve.wait_ge(r_ready, 1)
            copy_x(0, 0)
            copy_x(0, 1)
            hidden(0, 0)
            all_experts(dve, expert)

            def weighted(i):
                dve.wait_ge(f_first, i + 1)
                dve.scalar_tensor_tensor(y_sum[:, i], y_back[:, i, 1], w_tok[:, i, 1:2], y_sum[:, i],
                                         ALU.mult, ALU.add).then_inc(f_sum, 1)

            dve.wait_ge(gate_in[1], 16)
            weighted(0)
            for i in range(TILES + 1):
                if i + 1 < TILES:
                    weighted(i + 1)
                if i < TILES:
                    dve.wait_ge(f_sq, i + 1)
                    dve.tensor_scalar(stats[:, 6, i:i + 1], stats[:, 5, i:i + 1], 1.0 / D, EPS, ALU.mult, ALU.add).then_inc(f_ms, 1)
                if i:
                    dve.wait_ge(f_rs, i)
                    link(dve.scalar_tensor_tensor(y_sum[:, i - 1], y_sum[:, i - 1], stats[:, 7, i - 1:i],
                                                  gate_bc[:, 1, cond_of(i - 1), :], ALU.mult, ALU.mult))
                    dve.tensor_tensor(y_out[:, i - 1], res[:, i - 1], y_sum[:, i - 1], ALU.add).then_inc(f_out, 1)

        @block.scalar
        def _(act):
            act.wait_ge(s_zero, 1)
            act.wait_ge(s_rows, 128)
            act.activation(cond[:, :, 0:2], cond_in[:, :, :], ACT.Silu).then_inc(s_silu, 1)
            for i in range(TILES):
                act.wait_ge(s_xp if i == 0 else s_xs, 16)
                if i:
                    act.wait_ge(s_sq1, i)
                act.activation(junk_1[:], res[:, i], ACT.Square, accum_out=stats[:, 0, i:i + 1]).then_inc(s_sq1, 1)
            act.wait_ge(s_rs1, 1)
            for i in range(TILES):
                act.activation(res[:, i], res[:, i], ACT.Copy, scale=stats[:, 7, i:i + 1]).then_inc(s_xn, 1)
            for i in range(TILES):
                act.wait_ge(ht_tr, i + 1)
                act.copy(h_t[:, 4:KC, i * P:(i + 1) * P],
                         ps[:, 5 + 2 * (i % 2), :].rearrange("p (k q) -> p k q", q=P)).then_inc(ht_act, 1)
            act.wait_ge(s_pre1, 1)
            act.wait_ge(ht_act, TILES)
            for cn, (a, b) in enumerate(((0, P), (P, TILES * P))):
                for k in range(5, KC):
                    last = act.activation(h_t[:, k, a:b], h_t[:, k, a:b], ACT.Identity,
                                          bias=pre[:, 0, 1, k, cn:cn + 1], scale=pre[:, 0, 0, k, cn:cn + 1])
                last.then_inc(h_act, 1)

            def queries_out(i):
                act.wait_ge(qk_tr, i + 1)
                act.copy(q_t[:, :, i * P:(i + 1) * P], ps[:, 2, :].rearrange("p (g q) -> p g q", q=P)).then_inc(qk_act, 1)

            for i in range(TILES):
                act.wait_ge(qkv_mm, i + 1)
                if i >= 2:
                    act.wait_ge(rot_done, i - 1)
                if i == 2:
                    act.wait_ge(s_newkv, 16)
                bank = ps[:, 5 + 2 * (i % 2), :]
                act.copy(k_raw[:, i % 2], bank[:, 0:KVW])
                act.copy(v_all[:, 5 if i == 0 else i, :], bank[:, KVW:2 * KVW]).then_inc(kv_read, 1)
                if i == 0:
                    act.wait_ge(kv_read, 1)
                    act.dma_start(new_k[0, 0].rearrange("s h d -> s (h d)"), k_raw[:, 0]).then_inc(s_newkv, 16)
                    act.dma_start(new_v[0, 0].rearrange("s h d -> s (h d)"), v_all[:, 5, :]).then_inc(s_newkv, 16)
                    act.wait_ge(s_newkv, 32)
                else:
                    queries_out(i - 1)
            for u in range(2 * TILES):
                i = u % TILES
                act.wait_ge(gu_mm, u + 1)
                dst = gm_u[:, i] if u < TILES else gm_v[:, i]
                act.activation(dst, ps[:, 4 + u % 4, :], ACT.Gelu_apprx_tanh).then_inc(gelu_done, 1)
                if u == 0:
                    queries_out(TILES - 1)
                if u == TILES + 1:
                    act.wait_ge(ws_tr, 1)
                    act.copy(ws_t[:].rearrange("p (a h) q -> p a (h q)", a=2), ps[:, 0:2, :]).then_inc(ws_cp, 1)
                if u >= TILES:
                    act.wait_ge(gelu_done, u + 1)
                    if i == 0:
                        act.wait_ge(mod_tr, 5)
                        act.wait_ge(qk_tr, TILES)
                    if i >= 2:
                        act.wait_ge(gv_red, i - 1)
                    act.activation(sq[:, i % 2], gm_v[:, i], ACT.Square).then_inc(gsq_done, 1)
            for i in range(TILES):
                act.wait_ge(gm_tr, i + 1)
                act.copy(mix_t[:, PAIRS:KC, i * P:(i + 1) * P],
                         ps[:, 4 + i % 4, :].rearrange("p (k q) -> p k q", q=P)).then_inc(gm_cp, 1)

            NT = TILES * PAIRS
            MX, NM, SA, SUM, ES, DEN, INV = range(7)

            def width(t):
                i = t // PAIRS
                return P * (1 if i == 0 else 3 if i in (1, 4) else 4)

            def exps(t):
                act.wait_ge(sink_arg, t + 1)
                act.activation(att_stats[:, ES, t, :], att_stats[:, SA, t, :], ACT.Exp)
                if t >= 4:
                    act.wait_ge(pt_tr, 2 * (t - 4) + 2)
                for a in range(KVH):
                    last = act.activation(probs[:, t % 4, a, 0:width(t)], ps[:, 2 * (t % 2) + a, 0:width(t)], ACT.Exp,
                                          bias=att_stats[:, NM, t, a:a + 1], scale=SCALE,
                                          accum_out=att_stats[:, SUM, t, a:a + 1])
                last.then_inc(exp_done, 1)

            def p_out(t):
                act.wait_ge(pt_tr, 2 * t + 1)
                if t >= 4:
                    act.wait_ge(pv_mm, t // 2 - 1)
                w = width(t)
                act.copy(p_t[:, (t // 2) % 2, 0, 0:w // P, t % 2, :],
                         ps[:, 5 + (2 * t) % 3, 0:w].rearrange("p (x q) -> p x q", q=P)).then_inc(pt_even, 1)

            def values_out(m):
                act.wait_ge(pv_mm, m + 1)
                i, g = m // 2, 2 * (m % 2)
                act.copy(mix_t[:, g:g + 2, i * P:(i + 1) * P], ps[:, 4, 0:2 * P].rearrange("p (g q) -> p g q", q=P)).then_inc(pv_cp, 1)

            for t in range(NT + 3):
                if t < NT:
                    exps(t)
                if 2 <= t < NT + 2:
                    p_out(t - 2)
                if t >= 4 and t % 2 == 0:
                    values_out((t - 4) // 2)

            def norms(i):
                act.wait_ge(op_mm, i + 1)
                if i >= 2:
                    act.wait_ge(sq3, i - 1)
                act.activation(mix_g[:, i % 2].rearrange("p (a n) -> p a n", a=2), ps[:, 2 * (i % 2):2 * (i % 2) + 2, :], ACT.Square,
                               accum_out=stats[:, 2, i:i + 1]).then_inc(sq2, 1)
                if i:
                    scale_h2(i - 1)
                act.wait_ge(res1, i + 1)
                act.activation(mix_g[:, i % 2], res[:, i], ACT.Square, accum_out=stats[:, 5, i:i + 1]).then_inc(sq3, 1)
                act.wait_ge(rs3, i + 1)
                if i:
                    act.wait_ge(t2_tr, 2 * i)
                act.activation(xn2[:], res[:, i], ACT.Copy, scale=stats[:, 7, i:i + 1]).then_inc(xn2_done, 1)

            def scale_h2(i):
                cn = cond_of(i)
                act.wait_ge(t2_tr, 2 * i + 2)
                if i >= 2:
                    act.wait_ge(t2_back, 2 * i - 2)
                for k in range(4, KC):
                    last = act.activation(h2_t[:, i % 2, k, :], ps[:, 4 + (4 * i + 1) % 3, (k - 4) * P:(k - 3) * P],
                                          ACT.Identity, bias=pre[:, 1, 1, k, cn:cn + 1], scale=pre[:, 1, 0, k, cn:cn + 1])
                last.then_inc(t2_act, 1)

            def h2_back(i):
                act.wait_ge(rt_mm, i + 1)
                act.copy(lg_t[:, :], ps[0:GROUPS + EXPERTS, 7, 0:P]).then_inc(rt_cp, 1)
                act.wait_ge(t2_back, 2 * i + 2)
                if i >= 2:
                    act.wait_ge(h2_out[i % 2], 16 * (i // 2))
                act.copy(h2[:, i % 2, 512:1024], ps[:, 4 + (4 * i + 3) % 3, :]).then_inc(h2_act, 1)
                act.wait_ge(h2_act, i + 1)
                act.wait_ge(h2_dve, i + 1)
                act.dma_start(h2_dram[i * P:(i + 1) * P, :], h2[:, i % 2]).then_inc(h2_out[i % 2], 16)

            act.wait_ge(s_pre2, 1)
            for i in range(TILES):
                if i >= 2:
                    h2_back(i - 2)
                norms(i)
            h2_back(TILES - 2)
            scale_h2(TILES - 1)
            h2_back(TILES - 1)
            diff = r_e[:, 2:4].rearrange("p a n -> p (a n)")[:, 0:TILES * GROUPS]
            flat = lambda n: r_s[:, n].rearrange("p t k -> p (t k)")[:, 0:TILES]
            act.wait_ge(r_sub, 2 * TILES)
            act.activation(diff, diff, ACT.Exp).then_inc(r_exp, 1)
            act.activation(flat(6), flat(1), ACT.Exp).then_inc(r_exp, 1)

            def silu(q, c):
                e = q * WS + c
                act.wait_ge(gu2_mm, e + 1)
                if not below(e, 2):
                    act.wait_ge(hid_done, e - 1)
                act.activation(act_g[:, c % 2], ps[:, 2 + c % 2, 0:P], ACT.Silu).then_inc(silu_done, 1)

            def expert(q, c):
                e = q * WS + c
                if not isinstance(e, int) or e + 1 < EXPERTS:
                    silu(*nth(q, c, 1))
                act.wait_ge(ht2_tr, e + 1)
                if not below(e, 2):
                    act.wait_ge(y_mm, e - 1)
                act.copy(hid_t[:, c % 2], ps[:, 4 if c % 2 == 0 else 7, 0:P]).then_inc(ht2_cp, 1)
                act.wait_ge(y_mm, e + 1)
                if not below(e, XS):
                    act.wait_ge(y_st[c % XS], 16 * (q * (WS // XS) + c // XS))
                act.copy(y_buf(c), ps[:, 5 + c % 2, :]).then_inc(y_cp, 1)
                lo = act.value_load(extra_at[0:1, bass.ds(e, 1)], min_val=0, max_val=MAX_EXTRA)
                hi = act.value_load(extra_at[0:1, bass.ds(e + 1, 1)], min_val=0, max_val=MAX_EXTRA)
                with act.If(lo < hi), act.Fori(lo, hi) as x:
                    act.wait_ge(e_gu, x + 1)
                    act.activation(act_x[:, :], ps[:, 2 + c % 2, 0:P], ACT.Silu).then_inc(e_silu, 1)
                    act.wait_ge(e_htr, x + 1)
                    act.copy(hid_tx[:, :], ps[:, 4 if c % 2 == 0 else 7, 0:P]).then_inc(e_htc, 1)
                    act.wait_ge(e_y, x + 1)
                    act.copy(y_x[:, :], ps[:, 5 + c % 2, :]).then_inc(e_yc, 1)
                    act.wait_ge(e_st, 16 * (x + 1))

            act.wait_ge(r_ready, 1)
            silu(0, 0)
            all_experts(act, expert)

            def first_result(i):
                act.wait_ge(back_in[i], 16)
                act.activation(y_sum[:, i], y_back[:, i, 0], ACT.Copy, scale=w_tok[:, i, 0:1]).then_inc(f_first, 1)

            first_result(0)
            for i in range(TILES):
                if i + 1 < TILES:
                    first_result(i + 1)
                act.wait_ge(f_sum, i + 1)
                if i:
                    act.wait_ge(f_sq, i)
                act.activation(junk_3[:], y_sum[:, i], ACT.Square, accum_out=stats[:, 5, i:i + 1]).then_inc(f_sq, 1)

        @block.gpsimd
        def _(pool):
            pool.dma_start(v_all[:, 0, :], cache_v[0, 0].rearrange("s h d -> s (h d)")).then_inc(s_cv, 16)
            pool.dma_start(sink[:], attn_sink[0:1, :].broadcast_to((P, HEADS))).then_inc(s_small, 16)
            pool.dma_start(w_r[:, :, 0:GROUPS], router_group[0].rearrange("(k p) f -> p k f", p=P),
                           allow_slow_non_contiguous=True).then_inc(s_wr, 16)
            pool.dma_start(w_r[:, :, GROUPS:], router_expert[0].rearrange("(k p) f -> p k f", p=P)).then_inc(s_wr, 16)

            def rsqrt(dst, src, n, done):
                pool.tensor_tensor(dst, src, half_pow[:, 0:n], ALU.pow).then_inc(done, 1)

            pool.wait_ge(s_zero, 2)
            pool.wait_ge(s_ms1, 1)
            rsqrt(stats[:, 7, 0:TILES], stats[:, 1, 0:TILES], TILES, s_rs1)

            pool.wait_ge(ht_tr, TILES)
            pool.dma_start(ws_raw[:], gm_ws[0].rearrange("h p q -> p h q")).then_inc(s_ws, 16)
            pool.dma_start(gmn_bc[:], gm_norm.rearrange("a h d -> a (h d)").broadcast_to((P, GM))).then_inc(s_gmn, 16)

            pool.wait_ge(s_gmn, 16)
            for i in range(TILES + 1):
                if i < TILES:
                    pool.wait_ge(gv_ms, i + 1)
                    rsqrt(gm_stats[:, 2, i * GMH:(i + 1) * GMH], gm_stats[:, 1, i * GMH:(i + 1) * GMH], GMH, gv_rs)
                if i:
                    pool.wait_ge(gv_scaled, i)
                    pool.tensor_tensor(gm_v[:, i - 1], gm_v[:, i - 1], gmn_bc[:], ALU.mult).then_inc(gv_ready, 1)
            pool.wait_ge(pt_tr, 2 * TILES * PAIRS)
            pool.dma_start(res[:, 0, :], x_prompt[0]).then_inc(s_xre, 16)
            pool.dma_start(res[:, 1:TILES, :], x_lat).then_inc(s_xre, 16)

            for i in range(TILES):
                pool.wait_ge(ms2, i + 1)
                rsqrt(stats[:, 4, i:i + 1], stats[:, 3, i:i + 1], 1, rs2)
                pool.wait_ge(ms3, i + 1)
                rsqrt(stats[:, 7, i:i + 1], stats[:, 6, i:i + 1], 1, rs3)

            def gather(q, c):
                e, j = q * WS + c, c % XS
                pool.tensor_copy(idx_in[:, j, 0:1], src_row[:, bass.ds(e, 1)]).then_inc(idx_cp, 1)
                pool.wait_ge(idx_cp, e + 1)
                pool.sem_inc(idx_seen, 1)
                pool.indirect_dma_start(xg[:, j, :], None, h2_halves,
                                        bass.IndirectOffsetOnAxis(ap=idx_in[:, j, 0:1], axis=0),
                                        bounds_check=2 * TILES * P - 1, oob_is_err=False).then_inc(xg_in[j], 16)

            def scatter(q, c):
                e = q * WS + c
                pool.wait_ge(y_cp, e + 1)
                pool.tensor_copy(idx_out[:, c, 0:1], dst_row[:, bass.ds(e, 1)]).then_inc(out_idx, 1)
                pool.wait_ge(out_idx, e + 1)
                pool.sem_inc(idx_seen, 1)
                pool.indirect_dma_start(y_halves, bass.IndirectOffsetOnAxis(ap=idx_out[:, c, 0:1], axis=0),
                                        y_buf(c), None, bounds_check=2 * TOPK * TILES * P - 1,
                                        oob_is_err=False).then_inc(y_st[c % XS], 16)

            def gather_extra(x):
                pool.tensor_copy(idx_x[:, 0:1], src_row[:, bass.ds(EXPERTS + x, 1)]).then_inc(e_idx, 1)
                pool.wait_ge(e_idx, x + 1)
                pool.sem_inc(idx_seen, 1)
                pool.indirect_dma_start(xg_x[:, :], None, h2_halves,
                                        bass.IndirectOffsetOnAxis(ap=idx_x[:, 0:1], axis=0),
                                        bounds_check=2 * TILES * P - 1, oob_is_err=False).then_inc(e_in, 16)

            def extras(e):
                lo = pool.value_load(extra_at[0:1, bass.ds(e, 1)], min_val=0, max_val=MAX_EXTRA)
                hi = pool.value_load(extra_at[0:1, bass.ds(e + 1, 1)], min_val=0, max_val=MAX_EXTRA)
                with pool.If(lo < hi), pool.Fori(lo, hi) as x:
                    pool.wait_ge(e_tr, x + 1)
                    gather_extra(x + 1)
                    pool.wait_ge(e_yc, x + 1)
                    pool.tensor_copy(idx_xo[:, 0:1], dst_row[:, bass.ds(EXPERTS + x, 1)]).then_inc(e_out, 1)
                    pool.wait_ge(e_out, x + 1)
                    pool.sem_inc(idx_seen, 1)
                    pool.indirect_dma_start(y_halves, bass.IndirectOffsetOnAxis(ap=idx_xo[:, 0:1], axis=0),
                                            y_x[:, :], None, bounds_check=2 * TOPK * TILES * P - 1,
                                            oob_is_err=False).then_inc(e_st, 16)
                    pool.wait_ge(e_st, 16 * (x + 1))

            pool.wait_ge(r_ready, 1)
            pool.wait_ge(h2_out[0], 16 * 3)
            pool.wait_ge(h2_out[1], 16 * 2)
            pool.wait_ge(op_mm, TILES)
            for c in range(XS):
                gather(0, c)
            pool.memset(xg_x[:], 0.0).then_inc(xg_zero, 1)
            pool.wait_ge(xg_zero, 1)
            gather_extra(0)

            def gather_ahead(q, c):
                pool.wait_ge(x_tr, q * WS + c + 1)
                gather(*nth(q, c, XS))

            gather_ahead(0, 0)
            gather_ahead(0, 1)

            def expert(q, c):
                e = q * WS + c
                if not isinstance(e, int) or e + 2 + XS < EXPERTS:
                    gather_ahead(*nth(q, c, 2))
                scatter(q, c)
                extras(e)

            all_experts(pool, expert)
            pool.sem_inc(e_all, 1)
            n_extra = pool.value_load(extra_at[0:1, EXPERTS:EXPERTS + 1], min_val=0, max_val=MAX_EXTRA)
            pool.wait_ge(e_in, 16 * (n_extra + 1))

            for i in range(TILES):
                pool.wait_ge(f_ms, i + 1)
                rsqrt(stats[:, 7, i:i + 1], stats[:, 6, i:i + 1], 1, f_rs)


_INS = ['x_prompt', 'x_sample', 'cache_k', 'cache_v', 'c', 'c_ctx', 'w_mod', 'b_mod', 'g_pre_mix', 'w_in',
        'attn_sink', 'gm_norm', 'gm_ws', 'gm_b', 'w_out', 'g_post_mix', 'g_pre_ffn', 'router_group',
        'router_expert', 'w_gate', 'w_up', 'w_down', 'g_post_ffn']
_OUTS = [((1, CTX, D), 'float32'), ((1, LAT, D), 'float32'),
         ((1, 1, CTX, KVH, HD), 'float32'), ((1, 1, CTX, KVH, HD), 'float32')]


def kernel(**inputs):
    import numpy as _np
    import concourse.bacc as _bacc
    from concourse import mybir as _mybir
    from concourse.bass_utils import run_bass_kernel_spmd as _run

    nc = _bacc.Bacc("TRN2", target_bir_lowering=False, num_devices=1)
    arrays, args = {}, []
    for name in _INS + ["consts"]:
        a = constants() if name == "consts" else _np.ascontiguousarray(inputs[name])
        arrays[f"in_{name}_dram"] = a
        args.append(nc.dram_tensor(f"in_{name}_dram", a.shape, _mybir.dt.from_np(a.dtype), kind="ExternalInput").ap())
    for i, (shape, dtype) in enumerate(_OUTS):
        dt = _mybir.dt.from_np(_np.dtype(dtype))
        args.append(nc.dram_tensor(f"out_{i}_dram", shape, dt, kind="ExternalOutput").ap())
    hybrid_dit_step(nc, *args)
    r = _run(nc, [arrays], core_ids=[0])
    return tuple(r.results[0][f"out_{i}_dram"] for i in range(len(_OUTS)))
```
